# Optimizing a Trainium2 kernel written in Bass

```python
import jax, jax.numpy as jnp
from jax import lax
import numpy as np

D_MODEL = 1024
BATCH = 1
SEQ = 1024
DEPTH = 1

MIX_WIDTH = D_MODEL
RET_WIDTH = MIX_WIDTH // 2
RET_HEADS = 4
RET_HEAD_DIM = RET_WIDTH // RET_HEADS
SB_WIDTH = MIX_WIDTH - RET_WIDTH
SB_HEADS = 8
SB_HEAD_DIM = SB_WIDTH // SB_HEADS
IN_PROJ_WIDTH = 4 * RET_WIDTH + 3 * SB_WIDTH
RET_CHUNK = 128
SB_BLOCK = 128
ROPE_BASE = 10000.0
N_EXPERTS = 32
TOP_K = 4
D_FF = D_MODEL
SWIGLU_LIMIT = 7.0
SWIGLU_ALPHA = 1.702
MOE_BLOCK = 128
EPS = 1e-6

kernel_name = "hymba_retention_stickbreaking_moe"

def rmsnorm(x, g):
    xf = x.astype(jnp.float32)
    y = xf * lax.rsqrt(jnp.mean(xf * xf, axis=-1, keepdims=True) + EPS)
    return (y * g.astype(jnp.float32)).astype(x.dtype)

def rotary(x, pos):
    half = x.shape[-1] // 2
    inv_freq = ROPE_BASE ** (-jnp.arange(half, dtype=jnp.float32) / half)
    ang = pos.astype(jnp.float32)[:, None] * inv_freq[None, :]
    cos = jnp.cos(ang)[None, :, None, :]
    sin = jnp.sin(ang)[None, :, None, :]
    xf = x.astype(jnp.float32)
    x1, x2 = xf[..., :half], xf[..., half:]
    out = jnp.concatenate([x1 * cos - x2 * sin, x1 * sin + x2 * cos], axis=-1)
    return out.astype(x.dtype)

def retention_chunkwise(q, k, v):
    b, s, h, d = q.shape
    nc = s // RET_CHUNK
    log_gamma = jnp.log(1.0 - 2.0 ** (-5.0 - jnp.arange(h, dtype=jnp.float32)))
    idx = jnp.arange(RET_CHUNK, dtype=jnp.float32)
    diff = idx[:, None] - idx[None, :]
    intra = jnp.where(diff >= 0, jnp.exp(log_gamma[:, None, None] * jnp.maximum(diff, 0.0)), 0.0)
    q_decay = jnp.exp(log_gamma[:, None] * (idx + 1.0))
    k_decay = jnp.exp(log_gamma[:, None] * (RET_CHUNK - 1.0 - idx))
    chunk_decay = jnp.exp(log_gamma * RET_CHUNK)

    def to_chunks(t):
        return t.astype(jnp.float32).reshape(b, nc, RET_CHUNK, h, d).transpose(1, 0, 3, 2, 4)

    qc, kc, vc = to_chunks(q), to_chunks(k) * (d ** -0.5), to_chunks(v)

    def step(state, inp):
        qi, ki, vi = inp
        scores = jnp.einsum('bhnd,bhmd->bhnm', qi, ki) * intra[None]
        inner = jnp.einsum('bhnm,bhme->bhne', scores, vi)
        cross = jnp.einsum('bhnd,bhde->bhne', qi, state) * q_decay[None, :, :, None]
        new_state = state * chunk_decay[None, :, None, None] + jnp.einsum(
            'bhmd,bhme->bhde', ki * k_decay[None, :, :, None], vi)
        return new_state, inner + cross

    init = jnp.zeros((b, h, d, d), jnp.float32)
    _, out = lax.scan(step, init, (qc, kc, vc))
    return out.transpose(1, 0, 3, 2, 4).reshape(b, s, h, d).astype(q.dtype)

def stick_breaking_attention(q, k, v):
    b, s, h, d = q.shape
    nb = s // SB_BLOCK
    q_blocks = q.reshape(b, nb, SB_BLOCK, h, d).transpose(1, 0, 3, 2, 4)
    kt = k.transpose(0, 2, 1, 3)
    vt = v.transpose(0, 2, 1, 3)
    key_pos = jnp.arange(s)
    scale = d ** -0.5

    def block(args):
        q_blk, start = args
        z = jnp.einsum('bhqd,bhkd->bhqk', q_blk, kt).astype(jnp.float32) * scale
        q_pos = start + jnp.arange(SB_BLOCK)
        causal = key_pos[None, :] < q_pos[:, None]
        log_one_minus = jnp.where(causal, jax.nn.log_sigmoid(-z), 0.0)
        log_remaining = lax.cumsum(log_one_minus, axis=3, reverse=True) - log_one_minus
        weights = jnp.where(causal, jnp.exp(jax.nn.log_sigmoid(z) + log_remaining), 0.0)
        return jnp.einsum('bhqk,bhkd->bhqd', weights.astype(vt.dtype), vt)

    out = lax.map(block, (q_blocks, jnp.arange(nb) * SB_BLOCK))
    return out.transpose(1, 0, 3, 2, 4).reshape(b, s, h, d)

def hybrid_mixer(x, norm_g, w_in, ret_norm_g, sb_q_norm_g, sb_k_norm_g, w_out):
    b, s, _ = x.shape
    hx = rmsnorm(x, norm_g)
    proj = hx @ w_in
    splits = [RET_WIDTH * i for i in range(1, 5)] + [4 * RET_WIDTH + SB_WIDTH * i for i in range(1, 3)]
    rq, rk, rv, rg, sq, sk, sv = jnp.split(proj, splits, axis=-1)
    pos = jnp.arange(s)

    rq = rotary(rq.reshape(b, s, RET_HEADS, RET_HEAD_DIM), pos)
    rk = rotary(rk.reshape(b, s, RET_HEADS, RET_HEAD_DIM), pos)
    rv = rv.reshape(b, s, RET_HEADS, RET_HEAD_DIM)
    ret = rmsnorm(retention_chunkwise(rq, rk, rv), ret_norm_g)
    ret = ret.reshape(b, s, RET_WIDTH) * jax.nn.silu(rg)

    sq = rmsnorm(sq.reshape(b, s, SB_HEADS, SB_HEAD_DIM), sb_q_norm_g)
    sk = rmsnorm(sk.reshape(b, s, SB_HEADS, SB_HEAD_DIM), sb_k_norm_g)
    sv = sv.reshape(b, s, SB_HEADS, SB_HEAD_DIM)
    sb = stick_breaking_attention(sq, sk, sv).reshape(b, s, SB_WIDTH)

    mixed = jnp.concatenate([ret, sb.astype(ret.dtype)], axis=-1)
    return mixed @ w_out

def moe_ffn(x, norm_g, w_router, b_router, w_gate_up, b_gate_up, w_down, b_down):
    b, s, d = x.shape
    t = b * s
    xf = rmsnorm(x, norm_g).reshape(t, d)
    logits = (xf @ w_router + b_router).astype(jnp.float32)
    top_logits, top_idx = lax.top_k(logits, TOP_K)
    top_w = jax.nn.softmax(top_logits, axis=-1)

    n_assign = t * TOP_K
    flat_e = top_idx.reshape(-1)
    flat_tok = jnp.arange(n_assign, dtype=jnp.int32) // TOP_K
    flat_w = top_w.reshape(-1)
    order = jnp.argsort(flat_e, stable=True)
    sorted_e = flat_e[order]
    counts = jnp.bincount(flat_e, length=N_EXPERTS)
    starts = jnp.cumsum(counts) - counts
    padded = (counts + MOE_BLOCK - 1) // MOE_BLOCK * MOE_BLOCK
    padded_end = jnp.cumsum(padded)
    padded_start = padded_end - padded
    dest = padded_start[sorted_e] + jnp.arange(n_assign, dtype=jnp.int32) - starts[sorted_e]
    n_pad = n_assign + N_EXPERTS * MOE_BLOCK
    n_blocks = n_pad // MOE_BLOCK
    slot_tok = jnp.zeros((n_pad,), jnp.int32).at[dest].set(flat_tok[order])
    slot_w = jnp.zeros((n_pad,), jnp.float32).at[dest].set(flat_w[order])
    block_expert = jnp.minimum(
        jnp.searchsorted(padded_end, jnp.arange(n_blocks) * MOE_BLOCK, side='right'), N_EXPERTS - 1)
    x_slots = xf[slot_tok].reshape(n_blocks, MOE_BLOCK, d)

    def expert_block(args):
        xb, e = args
        gu = xb @ w_gate_up[e] + b_gate_up[e]
        gate = jnp.minimum(gu[:, 0::2], SWIGLU_LIMIT)
        up = jnp.clip(gu[:, 1::2], -SWIGLU_LIMIT, SWIGLU_LIMIT)
        hidden = (up + 1.0) * gate * jax.nn.sigmoid(SWIGLU_ALPHA * gate)
        return hidden @ w_down[e] + b_down[e]

    y_slots = lax.map(expert_block, (x_slots, block_expert)).reshape(n_pad, d)
    y = jax.ops.segment_sum(y_slots * slot_w[:, None].astype(y_slots.dtype), slot_tok, num_segments=t)
    return y.reshape(b, s, d).astype(x.dtype)

def setup_inputs(seed: int = 0) -> dict:
    key = jax.random.key(seed)
    ks = jax.random.split(key, 16)
    f32 = jnp.float32
    nrm = lambda k, shape, scale: jax.random.normal(k, shape, f32) * scale
    return {
        "x": nrm(ks[0], (BATCH, SEQ, D_MODEL), 1.0),
        "attn_norm_g": 1.0 + nrm(ks[1], (DEPTH, D_MODEL), 0.02),
        "w_in": nrm(ks[2], (DEPTH, D_MODEL, IN_PROJ_WIDTH), D_MODEL ** -0.5),
        "ret_norm_g": 1.0 + nrm(ks[3], (DEPTH, RET_HEADS, RET_HEAD_DIM), 0.02),
        "sb_q_norm_g": 1.0 + nrm(ks[4], (DEPTH, SB_HEAD_DIM), 0.02),
        "sb_k_norm_g": 1.0 + nrm(ks[5], (DEPTH, SB_HEAD_DIM), 0.02),
        "w_out": nrm(ks[6], (DEPTH, MIX_WIDTH, D_MODEL), MIX_WIDTH ** -0.5),
        "ffn_norm_g": 1.0 + nrm(ks[7], (DEPTH, D_MODEL), 0.02),
        "w_router": nrm(ks[8], (DEPTH, D_MODEL, N_EXPERTS), D_MODEL ** -0.5),
        "b_router": nrm(ks[9], (DEPTH, N_EXPERTS), 0.01),
        "w_gate_up": nrm(ks[10], (DEPTH, N_EXPERTS, D_MODEL, 2 * D_FF), D_MODEL ** -0.5),
        "b_gate_up": nrm(ks[11], (DEPTH, N_EXPERTS, 2 * D_FF), 0.02),
        "w_down": nrm(ks[12], (DEPTH, N_EXPERTS, D_FF, D_MODEL), D_FF ** -0.5),
        "b_down": nrm(ks[13], (DEPTH, N_EXPERTS, D_MODEL), 0.02),
    }

def reference(x, attn_norm_g, w_in, ret_norm_g, sb_q_norm_g, sb_k_norm_g, w_out,
              ffn_norm_g, w_router, b_router, w_gate_up, b_gate_up, w_down, b_down):
    for l in range(DEPTH):
        x = x + hybrid_mixer(x, attn_norm_g[l], w_in[l], ret_norm_g[l], sb_q_norm_g[l],
                             sb_k_norm_g[l], w_out[l])
        x = x + moe_ffn(x, ffn_norm_g[l], w_router[l], b_router[l], w_gate_up[l],
                        b_gate_up[l], w_down[l], b_down[l])
    return x


_drawn_inputs = setup_inputs


def setup_inputs(seed=0):
    import zlib

    import numpy as np

    out = dict(_drawn_inputs(seed))
    spreads = {}
    factors = {'sb_q_norm_g': 3.553,
     'sb_k_norm_g': 3.606,
     'b_gate_up': 5.857,
     'b_down': 6.631,
     'ret_norm_g': 3.289,
     'b_router': 3.039}
    for name, (base, spread) in spreads.items():
        noise = np.random.default_rng([zlib.crc32(name.encode()), seed]).standard_normal(out[name].shape)
        drawn = base * np.exp(spread * noise) if base else spread * noise
        out[name] = __import__('jax').numpy.asarray(drawn.astype(out[name].dtype))
    for name, factor in factors.items():
        out[name] = (out[name] * factor).astype(out[name].dtype)
    return out
```

```python
from contextlib import ExitStack

import numpy as np
import concourse.bass as bass
from concourse import mybir

F32 = mybir.dt.float32
U32 = mybir.dt.uint32
I32 = mybir.dt.int32
BF16 = mybir.dt.bfloat16
ALU = mybir.AluOpType
ACT = mybir.ActivationFunctionType
X = mybir.AxisListType.X

P = 128
S = 1024
D = 1024
NT = S // P
KD = D // P
RH = 4
SH = 8
HD = 64
NIN = 3584
CH = 512
NE = 32
CAP = 168
HC = CAP // 2
TOPK = 4
NB1 = -(-S // CAP) - 1
NX = TOPK * S // CAP + 1
NI = NE + NX
WIDTHS = (128, 136, 144, 152, 160)
IT_STEPS = 18
EPS = 1e-6
BIG = 1.0e30
GLIM = 7.0
GALPHA = 1.702

C_ID, C_NU, C_NO, C_MB, C_BO, C_LS, C_ON, C_CA = (P * i for i in range(8))
C_IO = 8 * P
C_I32 = C_IO + CAP
C_TID = C_I32 + NE
C_TIL = C_TID + NT
C_GV = C_TIL + NT
C_GO = C_GV + NT * RH
C_TH = C_GO + NT * RH
C_IX = C_TH + NB1
C_N = C_IX + NX
V_AG, V_FG, V_RG, V_SQ, V_SK, V_N = 0, 8, 16, 20, 21, 22


def constants():
    t = np.zeros((P, C_N), np.float32)
    r, c = np.arange(P)[:, None], np.arange(P)[None, :]
    t[:, C_ID:C_ID + P] = r == c
    t[:, C_NU:C_NU + P] = np.where(r >= c, -1.0, 0.0)
    t[:, C_NO:C_NO + P] = -1.0
    t[:, C_MB:C_MB + P] = np.where(r >= c, -BIG, 0.0)
    t[:, C_BO:C_BO + P] = (r // HD) == (c // HD)
    t[:, C_LS:C_LS + P] = r < c
    t[:, C_ON:C_ON + P] = 1.0
    t[:, C_CA:C_CA + P] = r <= c
    t[:, C_IO:C_IO + CAP] = np.arange(CAP)
    t[:, C_I32:C_I32 + NE] = np.arange(NE)
    tok = np.arange(NT)[None, :] * P + np.arange(P)[:, None]
    t[:, C_TID:C_TID + NT] = tok
    t[:, C_TIL:C_TIL + NT] = np.arange(NT) * P
    gamma = 1.0 - 2.0 ** (-5.0 - np.arange(RH, dtype=np.float64))
    g = np.log(gamma)[None, None, :]
    t[:, C_GV:C_GV + NT * RH] = np.exp(-(tok[:, :, None] + 1) * g).reshape(P, -1)
    t[:, C_GO:C_GO + NT * RH] = (np.exp((tok[:, :, None] + 1) * g) * P ** -0.5).reshape(P, -1)
    t[:, C_TH:C_TH + NB1] = CAP * (1 + np.arange(NB1))
    t[:, C_IX:C_IX + NX] = np.arange(NX)
    half = P // 2
    inv = (np.float32(10000.0) ** (-np.arange(half, dtype=np.float32) / np.float32(half))).astype(np.float32)
    ang = np.arange(S, dtype=np.float32)[None, :] * inv[:, None]
    cos, sin = np.cos(ang), np.sin(ang)
    rope = np.concatenate([np.concatenate([cos, cos]), np.concatenate([sin, -sin])], axis=1)
    return t, rope.astype(np.float32)


def layer(nc, x, attn_norm_g, w_in, ret_norm_g, sb_q_norm_g, sb_k_norm_g, w_out, ffn_norm_g,
          w_router, b_router, w_gate_up, b_gate_up, w_down, b_down, consts, rope, out):
    with ExitStack() as ctx:
        ctx.enter_context(nc.allow_non_contiguous_dma(reason="small vectors"))

        def sb(name, shape, dt=F32):
            return ctx.enter_context(nc.sbuf_tensor(name, shape, dt))

        def sem(name):
            return ctx.enter_context(nc.semaphore(name))

        ring = sb("ring", [P, 24576])
        hx = sb("hx", [P, 8192])
        mix = sb("mix", [P, 8192])
        work = sb("work", [P, 9728])
        cst = sb("cst", [P, C_N])
        small = sb("small", [P, 1000])
        bank = [ctx.enter_context(nc.psum_tensor(f"bank{i}", [P, 512], F32)) for i in range(8)]
        xn_dram = nc.dram_tensor("xn_scratch", [S, D], F32, kind="Internal").ap()

        ident = cst[:, C_ID:C_ID + P]
        neg_upper = cst[:, C_NU:C_NU + P]
        neg_ones = cst[:, C_NO:C_NO + P]
        mask_bias = cst[:, C_MB:C_MB + P]
        block_ones = cst[:, C_BO:C_BO + P]
        before = cst[:, C_LS:C_LS + P]
        ones = cst[:, C_ON:C_ON + P]
        causal = cst[:, C_CA:C_CA + P]
        iota_cap = cst[:, C_IO:C_IO + CAP]
        iota_e = cst[:, C_I32:C_I32 + NE]
        tok_id = cst[:, C_TID:C_TID + NT]
        tile_at = cst[:, C_TIL:C_TIL + NT]
        g_v = cst[:, C_GV:C_GV + NT * RH].rearrange("p (i h) -> p i h", h=RH)
        further = cst[:, C_TH:C_TH + NB1]
        iota_x = cst[:, C_IX:C_IX + NX]
        g_o = cst[:, C_GO:C_GO + NT * RH].rearrange("p (i h) -> p i h", h=RH)

        def region(t, at, *shape):
            n = int(np.prod(shape))
            v = t[:, at:at + n]
            if len(shape) == 1:
                return v
            names = "abcd"[:len(shape)]
            return v.rearrange(f"p ({' '.join(names)}) -> p {' '.join(names)}",
                               **{k: s for k, s in zip(names, shape)})

        rqT = region(ring, 0, RH, S)
        rkT = region(ring, 4096, RH, S)
        rv = region(ring, 8192, NT, CH)
        sqT = region(ring, 12288, 4, S)
        skT = region(ring, 16384, 4, S)
        sv = region(ring, 20480, NT, CH)
        x_in = [region(ring, 12288 + 1024 * i, D) for i in range(2)]
        square_dump = region(ring, 16384, D)
        x_norm = [region(ring, 20480 + 1024 * i, D) for i in range(2)]
        hxT = region(hx, 0, KD, S)
        wo = region(hx, 0, KD, D)
        mixT = region(mix, 0, KD, S)
        rope_t = region(mix, 0, 2, S)
        w_buf = [region(mix, 4096, KD, CH), region(work, 0, KD, CH)]
        k_tok = region(work, 4096, 2, CH)
        s_msk = region(work, 5120, 2, CH)
        state = region(work, 6144, CH)
        o_buf = region(work, 6656, 2, CH)
        o_sq = region(work, 7680, CH)
        prj_tmp = region(work, 8192, 2, CH)
        prj_std = region(work, 9216, CH)
        soft = region(work, 0, 3, CH)
        sp = region(work, 1536, 3, CH)
        wgt = region(work, 3072, 3, CH)
        later = region(work, 4608, 2, 2, CH)
        x_re = region(work, 0, 2, D)
        x2 = region(work, 2048, 2, D)
        xn2 = region(work, 4096, 2, D)
        xfT = region(work, 6144, 2, KD, P)
        e_dump = region(work, 8192, D)
        vec_rows = small[0:V_N, 0:P]
        vecs = small[:, 128:128 + V_N]
        sbq_g = small[:, 150:151]
        ssq = small[:, 152:160]
        ms = small[:, 160:168]
        rstd = small[:, 168:176]
        ret_ss = small[:, 176:192].rearrange("p (b h) -> p b h", h=RH)
        brt = small[:, 192:224]
        logits = region(small, 224, NT, NE)
        top_v = region(small, 480, NT, 8)
        top_i = region(small, 544, NT, 8)
        wr = region(small, 608, KD, NE)
        ssq2, ms2, rstd2 = small[:, 864:872], small[:, 872:880], small[:, 880:888]

        const_in = sem("const_in")
        vec_in = sem("vec_in")
        xt_in = [sem(f"xt_in{i}") for i in range(2)]
        win_in = [sem(f"win_in{i}") for i in range(2)]
        vec_tr = sem("vec_tr")
        vec_ok = sem("vec_ok")
        a_sq = sem("a_sq")
        a_ms = sem("a_ms")
        a_root = sem("a_root")
        a_inv = sem("a_inv")
        a_norm = sem("a_norm")
        a_tr = sem("a_tr")
        a_hx = sem("a_hx")
        prj = sem("prj")
        prj_free = sem("prj_free")
        rope_ok = sem("rope_ok")
        gate_sig = sem("gate_sig")
        qk_sq = sem("qk_sq")
        qk_sum = sem("qk_sum")
        qk_ms = sem("qk_ms")
        qk_root = sem("qk_root")
        qk_inv = sem("qk_inv")
        r_score = sem("r_score")
        r_ktr = sem("r_ktr")
        r_mask = sem("r_mask")
        r_k = sem("r_k")
        r_out = sem("r_out")
        r_acc = sem("r_acc")
        r_state = sem("r_state")
        r_o = sem("r_o")
        r_osq = sem("r_osq")
        r_ms = sem("r_ms")
        r_root = sem("r_root")
        r_inv = sem("r_inv")
        r_norm = sem("r_norm")
        r_tr = sem("r_tr")
        r_mix = sem("r_mix")
        wo_in = sem("wo_in")
        z_ok = sem("z_ok")
        z_abs = sem("z_abs")
        z_exp = sem("z_exp")
        z_ln = sem("z_ln")
        z_sp = sem("z_sp")
        z_cum = sem("z_cum")
        z_w = sem("z_w")
        z_zero = sem("z_zero")
        z_later = sem("z_later")
        z_pv = sem("z_pv")
        z_out = sem("z_out")
        xr_in = [sem(f"xr_in{i}") for i in range(2)]
        rt_in = sem("rt_in")
        e_prj = sem("e_prj")
        e_x2 = sem("e_x2")
        e_sq = sem("e_sq")
        e_ms = sem("e_ms")
        e_root = sem("e_root")
        e_inv = sem("e_inv")
        e_norm = sem("e_norm")
        e_st = [sem(f"e_st{i}") for i in range(2)]
        e_tr = sem("e_tr")
        e_xf = sem("e_xf")
        e_log = sem("e_log")
        e_logb = sem("e_logb")
        f_step = sem("f_step")
        f_exp = sem("f_exp")
        f_rank = sem("f_rank")
        it_step = sem("it_step")
        l_pos = sem("l_pos")
        pool_go = sem("pool_go")
        bias_in = sem("bias_in")
        bias_tr = sem("bias_tr")
        bias_ok = sem("bias_ok")
        gu_in = [sem(f"gu_in{c}") for c in range(4)]
        dn_in = [sem(f"dn_in{c}") for c in range(2)]
        l_hot = sem("l_hot")
        l_id = sem("l_id")
        l_sum = sem("l_sum")
        l_keep = sem("l_keep")
        l_ok = sem("l_ok")
        g_in = sem("g_in")
        g_tr = sem("g_tr")
        g_xT = sem("g_xT")
        m_bias = sem("m_bias")
        m_gu = sem("m_gu")
        m_gate = sem("m_gate")
        m_up = sem("m_up")
        m_sig = sem("m_sig")
        m_gs = sem("m_gs")
        m_hid = sem("m_hid")
        m_dn = sem("m_dn")
        m_y = sem("m_y")
        m_ytr = sem("m_ytr")
        m_yo = sem("m_yo")
        sc_done = sem("sc_done")

        block = ctx.enter_context(nc.Block())

        T_CHUNKS = (0, 1, 3, 4, 5)
        groups = [(c, s) for c in range(7) for s in range(8)]
        RSTEP = {33 + 2 * r: r for r in range(NT + 2)}
        units, chains = [], []
        for pair in range(SH // 2):
            for th in (1, 0):
                top = 4 * th + 3
                chains += [(2 * pair, th), (2 * pair + 1, th)]
                for b in range(top, -1, -1):
                    t0 = max(b * P, th * CH)
                    for par in range(2):
                        units.append(dict(h=2 * pair + par, th=th, b=b, par=par, t0=t0, o0=t0 - th * CH,
                                          diag=b * P >= th * CH, first=b == top, last=b == 0,
                                          step=top - b, chain=len(chains) - 2 + par))
        NU = len(units)

        hid = region(hx, 0, KD, CAP)
        xT = region(hx, 1344, KD, CAP)
        yT = region(hx, 2688, KD, CAP)
        hot = region(hx[:, 4032:4032 + NT * CAP // 2].bitcast(BF16), 0, NT, CAP)
        g1 = region(hx, 5376, 2, CAP)
        u1 = region(hx, 5712, 2, CAP)
        sg = region(hx, 6048, 2, CAP)
        gs = region(hx, 6384, 2, CAP)
        be = region(hx, 6720, 24)
        l_raw = region(hx, 6744, 2)[0:HC]
        idx = hx[0:HC, 6760:6762].bitcast(U32)
        wsel = hx[0:HC, 6762:6764]
        idx_sc = hx[0:HC, 6764:6766].bitcast(U32)
        w_sc = hx[0:HC, 6766:6768]
        btab = region(hx, 6784, NE, 24)
        pos_s = region(hx, 6768, NT)
        tw_s = region(hx[:, 7552:7552 + NT * 5 // 2].bitcast(BF16), 0, NT, 5)
        xg = region(mix, 0, 2, D)[0:HC]
        yo = region(mix, 2048, 2, D)[0:HC]
        pos = region(mix, 4096, NT, NE + 1)
        twx = region(mix[:, 4360:4360 + NT * (NE + 1) * 3 // 2].bitcast(BF16), 0, NT, NE + 1, 3)
        f_a = region(work, 0, NT, 4, NE)
        f_b = region(work, 1024, NT, 4, NE)
        f_m = region(work, 8192, NT, NE)
        f_r = region(work, 8448, NT, NE)
        f_c = region(work, 8704, NT, NE)
        f_w = region(work, 8960, NT, 4)
        f_s = region(work, 8992, NT)
        f_i = region(work, 9000, NT, 8)
        f_t = region(work, 9216, NT, NE)
        f_over = region(work, 9064, NE)
        f_cum = region(work, 9096, NE)
        f_cnt = region(work, 9128, NE)
        f_prior = region(work, 9160, NX)
        f_x = region(work, 0, NX, NE)
        f_y = region(work, 1024, NX, NE)
        it_base = region(mix, 5024, NI)
        it_low = region(mix, 5088, NI)
        it_f = region(mix, 5152, 2, NI)
        it_i = region(mix, 5280, 2, NI).bitcast(I32)
        b_rows = region(work, 4096, 3072)[0:NE]
        gu_ring = region(ring, 0, KD, 2048)
        dn_ring = region(ring, 16384, KD, D)

        xr = x[0].rearrange("(i p) d -> i p d", p=P)
        outr = out[0].rearrange("(i p) d -> i p d", p=P)
        out_rows = out[0]
        xnr = xn_dram.rearrange("(i p) d -> i p d", p=P)
        win_r = w_in[0].rearrange("(k p) (c n) -> c p k n", p=P, n=CH)
        gu_r = w_gate_up[0].rearrange("e (k p) (c n) -> e c p k n", p=P, n=512)
        dn_r = w_down[0].rearrange("e (k p) (c n) -> e c p k n", p=P, n=512)

        @block.sync
        def _(sp_eng):
            e = sp_eng
            for i in range(NT):
                if i >= 2:
                    e.wait_ge(a_norm, i - 1)
                e.dma_start(x_in[i % 2], xr[i]).then_inc(xt_in[i % 2], 16)
            for c in range(7):
                if c >= 2:
                    e.wait_ge(prj, 8 * (c - 1))
                e.dma_start(w_buf[c % 2], win_r[c]).then_inc(win_in[c % 2], 16)
            e.wait_ge(prj, 56)
            e.dma_start(wo, w_out[0].rearrange("(k p) n -> p k n", p=P)).then_inc(wo_in, 16)
            e.wait_ge(z_pv, NU)
            for c in range(4):
                e.dma_start(gu_ring[:, :, c * 512:(c + 1) * 512], gu_r[0, c]).then_inc(gu_in[c], 16)
            for c in range(2):
                e.dma_start(dn_ring[:, :, c * 512:(c + 1) * 512], dn_r[0, c]).then_inc(dn_in[c], 16)
            for i in range(NT):
                e.wait_ge(e_x2, 2 * i + 2)
                e.dma_start(outr[i], x2[:, i % 2]).then_inc(e_st[i % 2], 16)
                e.wait_ge(e_norm, i + 1)
                e.dma_start(xnr[i], xn2[:, i % 2]).then_inc(e_st[i % 2], 16)

            def load_expert(n, x_e):
                for c in range(4):
                    e.wait_ge(m_gu, n * 8 + (2 * c - 6))
                    e.dma_start(gu_ring[:, :, c * 512:(c + 1) * 512], gu_r[x_e, c]).then_inc(gu_in[c], 16)
                for c in range(2):
                    e.wait_ge(m_dn, n * 8 + (4 * c - 4))
                    e.dma_start(dn_ring[:, :, c * 512:(c + 1) * 512], dn_r[x_e, c]).then_inc(dn_in[c], 16)

            with e.Fori(1, NE) as n:
                load_expert(n, n)
            e.wait_ge(it_step, IT_STEPS)
            more = e.value_load(it_i[0:1, 1, NI - 1:NI], min_val=0, max_val=NX - 1)
            with e.If(more > 0):
                with e.Fori(NE, more + NE) as n:
                    load_expert(n, e.value_load(it_i[0:1, 0, bass.ds(n, 1)], min_val=0, max_val=NE - 1))

        @block.gpsimd
        def _(e):
            for g in range(16):
                c, s = groups[g]
                dst = (rqT if c == 0 else rkT)[:, s // 2, (s % 2) * CH:(s % 2 + 1) * CH]
                e.wait_ge(prj_free, g + 1)
                e.tensor_tensor(dst, dst, prj_tmp[:, g % 2], ALU.add).then_inc(rope_ok, 1)
            for c in range(NT):
                e.wait_ge(r_inv, c + 1)
                ob = o_buf[:, c % 2].rearrange("p (h n) -> p h n", h=RH)
                rs = ret_ss[:, 2 + c % 2, :]
                e.tensor_tensor(ob, ob, rs.unsqueeze(2).to_broadcast([P, RH, P]), ALU.mult).then_inc(r_norm, 1)
            e.wait_ge(r_mix, NT)
            e.wait_ge(prj_free, 56)
            for n, u in enumerate(units):
                lt = later[:, u["par"]]
                rng = slice(u["o0"], CH)
                if u["first"]:
                    if u["chain"] >= 2:
                        last = [m for m, w in enumerate(units) if w["chain"] == u["chain"] - 2][-1]
                        e.wait_ge(z_cum, last + 1)
                        e.wait_ge(z_later, last + 1)
                    e.memset(lt, 0.0).then_inc(z_zero, 1)
                    e.wait_ge(z_zero, u["chain"] + 1)
                elif n >= 2:
                    e.wait_ge(z_later, n - 1)
                    e.wait_ge(z_cum, n - 1)
                e.wait_ge(z_sp, n + 1)
                k = u["step"]
                e.tensor_tensor(lt[:, (k + 1) % 2, rng], lt[:, k % 2, rng], sp[:, n % 3, rng], ALU.add)\
                    .then_inc(z_later, 1)
            def gather():
                for h in range(2):
                    e.indirect_dma_start(out=xg[:, h], out_offset=None, in_=xn_dram,
                                         in_offset=bass.IndirectOffsetOnAxis(ap=idx[:, h:h + 1], axis=0)).then_inc(g_in, 16)

            e.wait_ge(e_log, NT)
            e.wait_ge(e_st[0], 128)
            e.wait_ge(e_st[1], 128)
            e.dma_start(b_rows[:, 2048:3072], b_down[0]).then_inc(sc_done, 16)
            e.wait_ge(l_ok, 1)
            e.wait_ge(e_st[0], 128)
            e.wait_ge(e_st[1], 128)
            e.wait_ge(e_prj, 16)
            gather()

            def add_rows(n):
                e.wait_ge(sc_done, n * 32 + 16)
                e.wait_ge(m_yo, n * 4 + 4)
                e.sem_inc(pool_go, 1)
                for h in range(2):
                    e.indirect_dma_start(out=out_rows, in_=yo[:, h], in_offset=None, compute_op=ALU.add,
                                         out_offset=bass.IndirectOffsetOnAxis(ap=idx_sc[:, h:h + 1], axis=0)).then_inc(sc_done, 16)

            def block_dmas(n):
                add_rows(n)
                e.wait_ge(l_ok, n + 2)
                e.wait_ge(g_tr, n * 3 + 3)
                e.sem_inc(pool_go, 1)
                gather()

            with e.Fori(0, NE) as n:
                block_dmas(n)
            e.wait_ge(sc_done, 32 * NE + 16)
            e.wait_ge(g_in, 32 * (NE + 1))
            e.wait_ge(it_step, IT_STEPS)
            more = e.value_load(it_i[0:1, 1, NI - 1:NI], min_val=0, max_val=NX - 1)
            with e.If(more > 0):
                with e.Fori(NE, more + NE) as n:
                    block_dmas(n)
                    e.wait_ge(sc_done, n * 32 + 48)
                    e.wait_ge(g_in, n * 32 + 64)
                    e.sem_inc(pool_go, 1)
            add_rows(more + NE)
            e.wait_ge(sc_done, more * 32 + (NE * 32 + 48))

        @block.scalar
        def _(e):
            e.dma_start(cst[:, :], consts).then_inc(const_in, 16)
            e.dma_start(rope_t, rope.rearrange("p (a n) -> p a n", a=2)).then_inc(const_in, 16)
            e.dma_start(vec_rows[V_AG:V_AG + 8], attn_norm_g[0].rearrange("(k p) -> k p", p=P)).then_inc(vec_in, 16)
            e.dma_start(vec_rows[V_FG:V_FG + 8], ffn_norm_g[0].rearrange("(k p) -> k p", p=P)).then_inc(vec_in, 16)
            e.dma_start(vec_rows[V_RG:V_RG + 4], ret_norm_g[0]).then_inc(vec_in, 16)
            for r, g in ((V_SQ, sb_q_norm_g), (V_SK, sb_k_norm_g)):
                for h in range(2):
                    e.dma_start(vec_rows[r:r + 1, h * HD:(h + 1) * HD], g).then_inc(vec_in, 16)
            e.dma_start(brt, b_router.to_broadcast([P, NE])).then_inc(rt_in, 16)
            e.dma_start(wr, w_router[0].rearrange("(k p) n -> p k n", p=P)).then_inc(rt_in, 16)
            for i in range(NT):
                e.wait_ge(xt_in[i % 2], 16 * (i // 2 + 1))
                if i:
                    e.wait_ge(a_sq, i)
                e.activation(square_dump, x_in[i % 2], ACT.Square, accum_out=ssq[:, i:i + 1]).then_inc(a_sq, 1)
                e.wait_ge(a_ms, i + 1)
                e.activation(ms[:, i:i + 1], ms[:, i:i + 1], ACT.Sqrt).then_inc(a_root, 1)
            for g, (c, s) in enumerate(groups):
                if c == 3:
                    e.wait_ge(prj, g + 1)
                    if g >= 26:
                        e.wait_ge(prj_free, g - 1)
                    if g == 24:
                        e.wait_ge(rope_ok, 16)
                    e.activation(prj_tmp[:, g % 2], bank[g % 3][:, :], ACT.Sigmoid).then_inc(gate_sig, 1)
                if c in (4, 5):
                    q = g - 32
                    e.wait_ge(prj, g + 1)
                    if q >= 2:
                        e.wait_ge(qk_sum, q - 1)
                    else:
                        e.wait_ge(prj_free, 32)
                    e.activation(prj_tmp[:, g % 2], bank[g % 3][:, :], ACT.Square).then_inc(qk_sq, 1)
                if 33 <= g <= 48:
                    e.wait_ge(qk_ms, g - 32)
                    e.activation(prj_std, prj_std, ACT.Sqrt).then_inc(qk_root, 1)
                if g in RSTEP:
                    r = RSTEP[g]
                    if 1 <= r <= NT:
                        cc = r - 1
                        e.wait_ge(r_acc, cc + 1)
                        e.activation(state, bank[7][:, :], ACT.Copy).then_inc(r_state, 1)
                        e.wait_ge(r_o, cc + 1)
                        if cc:
                            e.wait_ge(r_ms, 2 * cc)
                        e.activation(o_sq, o_buf[:, cc % 2], ACT.Square).then_inc(r_osq, 1)
                        e.wait_ge(r_ms, 2 * cc + 2)
                        e.activation(ret_ss[:, 2 + cc % 2, :], ret_ss[:, cc % 2, :], ACT.Sqrt).then_inc(r_root, 1)
                    if r < NT:
                        e.wait_ge(r_ktr, r + 1)
                        if r >= 2:
                            e.wait_ge(r_acc, r - 1)
                        e.activation(k_tok[:, r % 2], bank[4][:, :], ACT.Copy).then_inc(r_k, 1)

            def soft_plus(n):
                u = units[n]
                rng = slice(u["o0"], CH)
                e.wait_ge(z_ok, n + 1)
                if n >= 3:
                    e.wait_ge(z_sp, n - 2)
                e.activation(soft[:, n % 3, rng], bank[n % 4][:, rng], ACT.Abs).then_inc(z_abs, 1)
                e.wait_ge(z_abs, n + 1)
                e.activation(soft[:, n % 3, rng], soft[:, n % 3, rng], ACT.Exp, scale=-1.0).then_inc(z_exp, 1)
                e.wait_ge(z_exp, n + 1)
                e.activation(soft[:, n % 3, rng], soft[:, n % 3, rng], ACT.Ln, bias=1.0).then_inc(z_ln, 1)

            def weights(n):
                u = units[n]
                rng = slice(u["o0"], CH)
                e.wait_ge(z_cum, n + 1)
                if n >= 3:
                    e.wait_ge(z_pv, n - 2)
                e.activation(wgt[:, n % 3, rng], bank[n % 4][:, rng], ACT.Exp).then_inc(z_w, 1)

            e.wait_ge(r_mix, NT)
            e.preload_act_table_set("natural_log_exp_and_others")
            for n in range(NU + 2):
                if n < NU:
                    soft_plus(n)
                if n >= 2:
                    weights(n - 2)
            e.wait_ge(z_pv, NU)
            e.wait_ge(z_later, NU)
            for i in range(2):
                e.dma_start(x_re[:, i], xr[i]).then_inc(xr_in[i], 16)
            for i in range(NT):
                e.wait_ge(e_x2, 2 * i + 2)
                if i + 2 < NT:
                    e.dma_start(x_re[:, i % 2], xr[i + 2]).then_inc(xr_in[i % 2], 16)
                if i:
                    e.wait_ge(e_sq, i)
                e.activation(e_dump, x2[:, i % 2], ACT.Square, accum_out=ssq2[:, i:i + 1]).then_inc(e_sq, 1)
                e.wait_ge(e_ms, i + 1)
                e.activation(ms2[:, i:i + 1], ms2[:, i:i + 1], ACT.Sqrt).then_inc(e_root, 1)
                e.wait_ge(e_inv, i + 1)
                if i >= 2:
                    e.wait_ge(e_tr, 2 * (i - 1))
                    e.wait_ge(e_st[i % 2], 32 * (i // 2))
                e.activation(xn2[:, i % 2], x2[:, i % 2], ACT.Copy, scale=rstd2[:, i:i + 1]).then_inc(e_norm, 1)
            e.wait_ge(f_step, 1)
            e.activation(f_w, f_w, ACT.Exp).then_inc(f_exp, 1)
            e.wait_ge(e_log, NT)
            e.wait_ge(e_st[0], 128)
            e.wait_ge(e_st[1], 128)
            e.dma_start(b_rows[:, 0:2048], b_gate_up[0]).then_inc(bias_in, 16)

            def weigh_rows(n):
                e.wait_ge(sc_done, n * 32 + 16)
                for h in range(2):
                    for q in range(2):
                        m = 2 * h + q
                        e.wait_ge(m_ytr, n * 4 + (m + 1))
                        e.activation(yo[:, h, q * 512:(q + 1) * 512], bank[4 + m][0:HC, :], ACT.Copy,
                                     scale=w_sc[:, h:h + 1]).then_inc(m_yo, 1)

            def block_act(n):
                for f in range(KD):
                    e.wait_ge(m_gate, n * 8 + (f + 1))
                    e.wait_ge(m_gs, n * 8 + (f + 1))
                    e.activation(sg[:, f % 2], g1[:, f % 2], ACT.Sigmoid, scale=GALPHA).then_inc(m_sig, 1)
                    if f == 0:
                        weigh_rows(n)

            with e.Fori(0, NE) as n:
                block_act(n)
            more = e.value_load(it_i[0:1, 1, NI - 1:NI], min_val=0, max_val=NX - 1)
            with e.If(more > 0):
                with e.Fori(NE, more + NE) as n:
                    block_act(n)
            weigh_rows(more + NE)

        @block.tensor
        def _(e):
            e.wait_ge(const_in, 32)
            e.wait_ge(vec_in, 16 * 7)
            e.transpose(bank[3][:, 0:V_N], vec_rows, cst[0:V_N, C_ID:C_ID + V_N]).then_inc(vec_tr, 1)
            for i in range(NT):
                e.wait_ge(a_norm, i + 1)
                for hf in range(2):
                    m = 2 * i + hf
                    if m >= 4:
                        e.wait_ge(a_hx, m - 3)
                    for q in range(4):
                        mm = e.transpose(bank[4 + m % 4][:, q * P:(q + 1) * P],
                                         x_norm[i % 2][:, (4 * hf + q) * P:(4 * hf + q + 1) * P], ident)
                    mm.then_inc(a_tr, 1)

            def project(g):
                c, s = groups[g]
                w = w_buf[c % 2]
                if s == 0:
                    e.wait_ge(win_in[c % 2], 16 * (c // 2 + 1))
                if g == 0:
                    e.wait_ge(a_hx, 16)
                if g >= 3:
                    e.wait_ge(prj_free, g - 2)
                for k in range(KD):
                    if c in T_CHUNKS:
                        lhs, rhs = w[:, k, (s // 2) * P:(s // 2 + 1) * P], hxT[:, k, (s % 2) * CH:(s % 2 + 1) * CH]
                    else:
                        lhs, rhs = hxT[:, k, s * P:(s + 1) * P], w[:, k, :]
                    mm = e.matmul(bank[g % 3][:, :], lhs, rhs, start=k == 0, stop=k == KD - 1)
                mm.then_inc(prj, 1)

            def head_sums(q):
                e.wait_ge(qk_sq, q + 1)
                if q:
                    e.wait_ge(qk_ms, q)
                e.matmul(bank[3][:, :], block_ones, prj_tmp[:, q % 2], start=True, stop=True).then_inc(qk_sum, 1)

            def retention(r):
                if 2 <= r:
                    c = r - 2
                    e.wait_ge(r_norm, c + 1)
                    e.wait_ge(r_k, min(r, NT))
                    for h in range(RH):
                        mm = e.transpose(bank[4][:, h * P:(h + 1) * P], o_buf[:, c % 2, h * P:(h + 1) * P], ident)
                    mm.then_inc(r_tr, 1)
                if 1 <= r <= NT:
                    c = r - 1
                    e.wait_ge(r_mask, c + 1)
                    e.wait_ge(r_k, c + 1)
                    if c:
                        e.wait_ge(r_o, c)
                        e.wait_ge(r_state, c)
                    for h in range(RH):
                        o = bank[6][:, h * P:(h + 1) * P]
                        mm = e.matmul(o, s_msk[:, c % 2, h * P:(h + 1) * P], rv[:, c, h * P:(h + 1) * P],
                                      start=True, stop=c == 0)
                        if c:
                            mm = e.matmul(o, rqT[:, h, c * P:(c + 1) * P], state[:, h * P:(h + 1) * P],
                                          start=False, stop=True)
                    mm.then_inc(r_out, 1)
                    for h in range(RH):
                        mm = e.matmul(bank[7][:, h * P:(h + 1) * P], k_tok[:, c % 2, h * P:(h + 1) * P],
                                      rv[:, c, h * P:(h + 1) * P], start=c == 0 and h == 0, stop=True,
                                      skip_group_check=True)
                    mm.then_inc(r_acc, 1)
                if r < NT:
                    if r == 0:
                        e.wait_ge(rope_ok, 16)
                        e.wait_ge(prj_free, 24)
                    else:
                        e.wait_ge(r_mask, r)
                    for h in range(RH):
                        mm = e.matmul(bank[5][:, h * P:(h + 1) * P], rkT[:, h, r * P:(r + 1) * P],
                                      rqT[:, h, r * P:(r + 1) * P], start=True, stop=True)
                    mm.then_inc(r_score, 1)
                    if r >= 2:
                        e.wait_ge(r_mix, r - 1)
                    elif r:
                        e.wait_ge(r_k, r)
                    for h in range(RH):
                        mm = e.transpose(bank[4][:, h * P:(h + 1) * P], rkT[:, h, r * P:(r + 1) * P], ident)
                    mm.then_inc(r_ktr, 1)

            for g in range(len(groups)):
                project(g)
                if 33 <= g <= 48:
                    head_sums(g - 33)
                if g in RSTEP:
                    retention(RSTEP[g])

            def score_unit(n):
                u = units[n]
                pr = slice(HD * (u["h"] % 2), HD * (u["h"] % 2) + HD)
                if n >= 4:
                    e.wait_ge(z_w, n - 3)
                mm = e.matmul(bank[n % 4][:, u["o0"]:CH], skT[pr, u["h"] // 2, u["b"] * P:(u["b"] + 1) * P],
                              sqT[pr, u["h"] // 2, u["t0"]:(u["th"] + 1) * CH], start=True, stop=False,
                              skip_group_check=True)
                if u["diag"]:
                    mm = e.matmul(bank[n % 4][:, u["o0"]:u["o0"] + P], ident, mask_bias, start=False,
                                  stop=False, skip_group_check=True)
                mm.then_inc(z_ok, 1)

            def cumulate(n):
                u = units[n]
                e.wait_ge(z_sp, n + 1)
                mm = e.matmul(bank[n % 4][:, u["o0"]:CH], neg_upper, sp[:, n % 3, u["o0"]:CH], start=False,
                              stop=u["first"], skip_group_check=True)
                if not u["first"]:
                    e.wait_ge(z_later, n - 1)
                    mm = e.matmul(bank[n % 4][:, u["o0"]:CH], neg_ones, later[:, u["par"], u["step"] % 2, u["o0"]:CH],
                                  start=False, stop=True, skip_group_check=True)
                mm.then_inc(z_cum, 1)

            def values(n):
                u = units[n]
                pr = slice(HD * (u["h"] % 2), HD * (u["h"] % 2) + HD)
                e.wait_ge(z_w, n + 1)
                if u["first"] and u["chain"] >= 4:
                    e.wait_ge(z_out, u["chain"] - 3)
                e.matmul(bank[4 + u["chain"] % 4][pr, u["o0"]:CH], sv[:, u["b"], u["h"] * HD:(u["h"] + 1) * HD],
                         wgt[:, n % 3, u["o0"]:CH], start=u["first"], stop=u["last"],
                         skip_group_check=True).then_inc(z_pv, 1)

            e.wait_ge(prj_free, 56)
            e.wait_ge(r_mix, NT)
            e.wait_ge(r_state, NT)
            for n in range(-2, NU + 2):
                if 0 <= n + 2 < NU:
                    score_unit(n + 2)
                if 0 <= n < NU:
                    cumulate(n)
                if n >= 2:
                    values(n - 2)

            e.wait_ge(wo_in, 16)
            e.wait_ge(z_out, 16)
            e.wait_ge(rt_in, 32)

            def out_proj(i):
                for nh in range(2):
                    g = 2 * i + nh
                    if g >= 4:
                        e.wait_ge(e_x2, g - 3)
                    for k in range(KD):
                        mm = e.matmul(bank[g % 4][:, :], mixT[:, k, i * P:(i + 1) * P],
                                      wo[:, k, nh * CH:(nh + 1) * CH], start=k == 0, stop=k == KD - 1)
                    mm.then_inc(e_prj, 1)

            def turn(i):
                e.wait_ge(e_norm, i + 1)
                for hf in range(2):
                    if i:
                        e.wait_ge(e_xf, 2 * i - 1 + hf)
                    for q in range(4):
                        k = 4 * hf + q
                        mm = e.transpose(bank[4 + hf][:, q * P:(q + 1) * P], xn2[:, i % 2, k * P:(k + 1) * P], ident)
                    mm.then_inc(e_tr, 1)

            def route(i):
                e.wait_ge(e_xf, 2 * i + 2)
                if i:
                    e.wait_ge(e_logb, 3 * i - 2)
                for k in range(KD):
                    mm = e.matmul(bank[6][:, 0:NE], xfT[:, i % 2, k, :], wr[:, k, :], start=k == 0, stop=k == KD - 1)
                mm.then_inc(e_log, 1)

            for i in range(NT + 2):
                if i < NT:
                    out_proj(i)
                if 1 <= i <= NT:
                    turn(i - 1)
                if 2 <= i:
                    route(i - 2)
            e.wait_ge(bias_in, 16)
            e.wait_ge(sc_done, 16)
            e.wait_ge(e_x2, 16)
            for j in range(24):
                if j < 16:
                    src = b_rows[:, (j % 8) * 256 + j // 8:(j % 8) * 256 + 256:2]
                else:
                    src = b_rows[:, 2048 + (j - 16) * P:2048 + (j - 15) * P]
                mm = e.transpose(bank[j // 12][:, (j % 12) * NE:(j % 12 + 1) * NE], src, cst[0:NE, C_ID:C_ID + NE])
            mm.then_inc(bias_tr, 1)
            e.wait_ge(f_step, 4)
            e.matmul(bank[2][:, 0:NT * NE], before, f_m.rearrange("p i e -> p (i e)"), start=True, stop=False,
                     skip_group_check=True)
            for j in range(NT - 1):
                n = NT - 1 - j
                mm = e.matmul(bank[2][:, (j + 1) * NE:NT * NE].rearrange("p (i e) -> p i e", e=NE), ones,
                              f_m[:, j:j + 1, :].to_broadcast([P, n, NE]), start=False, stop=j == NT - 2,
                              skip_group_check=True)
            for j in range(NT):
                mm = e.matmul(bank[3][:, 0:NE], ones, f_m[:, j, :], start=j == 0, stop=j == NT - 1)
            mm.then_inc(f_rank, 1)

            def token_list():
                for h in range(2):
                    for i in range(NT):
                        mm = e.matmul(bank[7][0:HC, 5 * h:5 * h + 5], hot[:, i, h * HC:(h + 1) * HC], tw_s[:, i, :],
                                      start=i == 0, stop=i == NT - 1)
                mm.then_inc(l_sum, 1)

            def turn_tokens():
                for k in range(KD):
                    for h in range(2):
                        at = (k % 3) * CAP + h * HC
                        mm = e.transpose(bank[4 + k // 3][:, at:at + HC], xg[:, h, k * P:(k + 1) * P],
                                         cst[0:HC, C_ID:C_ID + HC])
                    if k in (2, 5, 7):
                        mm.then_inc(g_tr, 1)

            e.wait_ge(l_hot, 1)
            token_list()
            e.wait_ge(bias_ok, 3)
            e.wait_ge(g_in, 32)
            turn_tokens()

            def turn_rows(n):
                e.wait_ge(m_y, n * 8 + 2)
                e.wait_ge(l_ok, n + 1)
                for h in range(2):
                    for q in range(2):
                        for r in range(4):
                            mm = e.transpose(bank[4 + 2 * h + q][0:HC, r * P:(r + 1) * P],
                                             yT[:, 4 * q + r, h * HC:(h + 1) * HC], ident)
                        mm.then_inc(m_ytr, 1)

            def block_matmuls(n, w):
                e.wait_ge(g_xT, n * 3 + 3)
                for f in range(KD):
                    if f % 2 == 0:
                        e.wait_ge(gu_in[f // 2], n * 16 + 16)
                    e.wait_ge(m_up, n * 8 + (f + 1))
                    for part in range(2):
                        for k in range(KD):
                            mm = e.matmul(bank[f % 2][:, part * CAP:part * CAP + w],
                                          gu_ring[:, k, f * 256 + part:(f + 1) * 256:2], xT[:, k, 0:w],
                                          start=k == 0, stop=k == KD - 1)
                    mm.then_inc(m_gu, 1)
                    if f == 0:
                        turn_rows(n)
                    if f == 5:
                        e.wait_ge(l_hot, n + 2)
                        e.wait_ge(m_yo, n * 4 + 4)
                        token_list()
                def down(j, k):
                    return e.matmul(bank[2 + j % 2][:, 0:w], dn_ring[:, k, j * P:(j + 1) * P], hid[:, k, 0:w],
                                    start=k == 0, stop=k == KD - 1)

                e.wait_ge(dn_in[0], n * 16 + 16)
                e.wait_ge(m_hid, n * 8 + 9)
                for j in range(2):
                    e.wait_ge(m_y, n * 8 + (j + 1))
                    for k in range(KD - 1):
                        down(j, k)
                for j in range(KD):
                    if j < 2:
                        e.wait_ge(m_hid, n * 8 + 10)
                        down(j, KD - 1).then_inc(m_dn, 1)
                        continue
                    if j == 4:
                        e.wait_ge(dn_in[1], n * 16 + 16)
                    e.wait_ge(m_y, n * 8 + (j + 1))
                    for k in range(KD):
                        mm = down(j, k)
                    mm.then_inc(m_dn, 1)
                    if j == 5:
                        e.wait_ge(g_in, n * 32 + 64)
                        e.wait_ge(m_yo, n * 4 + 4)
                        turn_tokens()

            def block_pe(n):
                tokens = e.value_load(it_i[0:1, 1, bass.ds(n, 1)], min_val=-S, max_val=S)

                def choose(widths):
                    if not widths:
                        block_matmuls(n, CAP)
                        return
                    with e.If(tokens <= widths[0]):
                        block_matmuls(n, widths[0])
                    with e.Else():
                        choose(widths[1:])

                choose(WIDTHS)

            e.wait_ge(it_step, 1)
            with e.Fori(0, NE) as n:
                block_pe(n)
            more = e.value_load(it_i[0:1, 1, NI - 1:NI], min_val=0, max_val=NX - 1)
            with e.If(more > 0):
                with e.Fori(NE, more + NE) as n:
                    block_pe(n)
            turn_rows(more + NE)

        @block.vector
        def _(e):
            e.wait_ge(vec_tr, 1)
            e.tensor_copy(vecs, bank[3][:, 0:V_N]).then_inc(vec_ok, 1)
            e.wait_ge(vec_ok, 1)
            e.tensor_scalar(sbq_g, vecs[:, V_SQ:V_SQ + 1], HD ** -0.5, None, ALU.mult).then_inc(vec_ok, 1)

            def to_hx(i):
                for hf in range(2):
                    e.wait_ge(a_tr, 2 * i + hf + 1)
                    g = vecs[:, V_AG + 4 * hf:V_AG + 4 * hf + 4]
                    e.tensor_tensor(hxT[:, 4 * hf:4 * hf + 4, i * P:(i + 1) * P],
                                    bank[4 + (2 * i + hf) % 4][:, :].rearrange("p (k t) -> p k t", t=P),
                                    g.unsqueeze(2).to_broadcast([P, 4, P]), ALU.mult).then_inc(a_hx, 1)

            for i in range(NT):
                e.wait_ge(a_sq, i + 1)
                e.tensor_scalar(ms[:, i:i + 1], ssq[:, i:i + 1], 1.0 / D, EPS, ALU.mult, ALU.add).then_inc(a_ms, 1)
                e.wait_ge(a_root, i + 1)
                e.reciprocal(rstd[:, i:i + 1], ms[:, i:i + 1]).then_inc(a_inv, 1)
                e.wait_ge(a_inv, i + 1)
                if i >= 2:
                    e.wait_ge(a_tr, 2 * i - 2)
                e.tensor_scalar(x_norm[i % 2], x_in[i % 2], rstd[:, i:i + 1], None, ALU.mult).then_inc(a_norm, 1)
                if i:
                    to_hx(i - 1)
            to_hx(NT - 1)

            def qk_mean(q):
                e.wait_ge(qk_sum, q + 1)
                if q:
                    e.wait_ge(prj_free, 32 + q)
                e.tensor_scalar(prj_std, bank[3][:, :], 1.0 / HD, EPS, ALU.mult, ALU.add).then_inc(qk_ms, 1)

            def qk_norm(q):
                g = q + 32
                c, s = groups[g]
                dst = (sqT if c == 4 else skT)[:, s // 2, (s % 2) * CH:(s % 2 + 1) * CH]
                gv = sbq_g if c == 4 else vecs[:, V_SK:V_SK + 1]
                e.wait_ge(qk_root, q + 1)
                e.reciprocal(prj_std, prj_std).then_inc(qk_inv, 1)
                e.wait_ge(qk_inv, q + 1)
                e.scalar_tensor_tensor(dst, bank[g % 3][:, :], gv, prj_std, ALU.mult, ALU.mult).then_inc(prj_free, 1)

            def retention(r):
                if 1 <= r <= NT:
                    c = r - 1
                    e.wait_ge(r_out, c + 1)
                    if c >= 2:
                        e.wait_ge(r_tr, c - 1)
                    e.tensor_tensor(o_buf[:, c % 2].rearrange("p (h n) -> p h n", h=RH),
                                    bank[6][:, :].rearrange("p (h n) -> p h n", h=RH),
                                    g_o[:, c, :].unsqueeze(2).to_broadcast([P, RH, P]), ALU.mult).then_inc(r_o, 1)
                if r < NT:
                    e.wait_ge(r_score, r + 1)
                    if r >= 2:
                        e.wait_ge(r_out, r - 1)
                    e.tensor_tensor(s_msk[:, r % 2].rearrange("p (h n) -> p h n", h=RH),
                                    bank[5][:, :].rearrange("p (h n) -> p h n", h=RH),
                                    causal.unsqueeze(1).to_broadcast([P, RH, P]), ALU.mult).then_inc(r_mask, 1)
                if 2 <= r:
                    c = r - 2
                    e.wait_ge(r_tr, c + 1)
                    dst = mixT[:, 0:RH, c * P:(c + 1) * P]
                    e.tensor_tensor(dst, bank[4][:, :].rearrange("p (h n) -> p h n", h=RH), dst,
                                    ALU.mult).then_inc(r_mix, 1)
                if 1 <= r <= NT:
                    c = r - 1
                    e.wait_ge(r_osq, c + 1)
                    if c >= 2:
                        e.wait_ge(r_root, c - 1)
                    e.tensor_reduce(ret_ss[:, c % 2, :], o_sq.rearrange("p (h n) -> p h n", h=RH), X, ALU.add).then_inc(r_ms, 1)
                    e.wait_ge(r_ms, 2 * c + 1)
                    e.tensor_scalar(ret_ss[:, c % 2, :], ret_ss[:, c % 2, :], 1.0 / P, EPS, ALU.mult, ALU.add).then_inc(r_ms, 1)
                    e.wait_ge(r_root, c + 1)
                    e.reciprocal(ret_ss[:, 2 + c % 2, :], ret_ss[:, 2 + c % 2, :]).then_inc(r_inv, 1)

            for g, (c, s) in enumerate(groups):
                src = bank[g % 3][:, :]
                if c in (0, 1):
                    dst = (rqT if c == 0 else rkT)[:, s // 2, (s % 2) * CH:(s % 2 + 1) * CH]
                    ts = slice((s % 2) * CH, (s % 2 + 1) * CH)
                    t = prj_tmp[:, g % 2]
                    e.wait_ge(prj, g + 1)
                    if g == 0:
                        e.wait_ge(const_in, 32)
                    if g >= 2:
                        e.wait_ge(rope_ok, g - 1)
                    e.tensor_tensor(t[0:64], src[64:128], rope_t[64:128, 1, ts], ALU.mult)
                    e.tensor_tensor(t[64:128], src[0:64], rope_t[0:64, 1, ts], ALU.mult)
                    e.tensor_tensor(dst, src, rope_t[:, 0, ts], ALU.mult).then_inc(prj_free, 1)
                elif c == 2:
                    e.wait_ge(prj, g + 1)
                    e.tensor_tensor(rv[:, s, :].rearrange("p (h n) -> p h n", h=RH),
                                    src.rearrange("p (h n) -> p h n", h=RH),
                                    g_v[:, s, :].unsqueeze(2).to_broadcast([P, RH, P]), ALU.mult).then_inc(prj_free, 1)
                elif c == 3:
                    e.wait_ge(gate_sig, g - 23)
                    e.scalar_tensor_tensor(mixT[:, s // 2, (s % 2) * CH:(s % 2 + 1) * CH], src,
                                           vecs[:, V_RG + s // 2:V_RG + s // 2 + 1], prj_tmp[:, g % 2],
                                           ALU.mult, ALU.mult).then_inc(prj_free, 1)
                if 33 <= g <= 48:
                    qk_mean(g - 33)
                    qk_norm(g - 33)
                if c == 6:
                    e.wait_ge(prj, g + 1)
                    e.tensor_copy(sv[:, s, :], src).then_inc(prj_free, 1)
                if g in RSTEP:
                    retention(RSTEP[g])


            def softplus(n):
                u = units[n]
                rng = slice(u["o0"], CH)
                e.wait_ge(z_ln, n + 1)
                if n >= 3:
                    e.wait_ge(z_cum, n - 2)
                    e.wait_ge(z_later, n - 2)
                e.scalar_tensor_tensor(sp[:, n % 3, rng], bank[n % 4][:, rng], 0.0, soft[:, n % 3, rng],
                                       ALU.max, ALU.add).then_inc(z_sp, 1)

            def chain_out(n):
                u = units[n]
                pr = slice(HD * (u["h"] % 2), HD * (u["h"] % 2) + HD)
                e.wait_ge(z_pv, n + 1)
                e.tensor_copy(mixT[pr, RH + u["h"] // 2, u["th"] * CH:(u["th"] + 1) * CH],
                              bank[4 + u["chain"] % 4][pr, :]).then_inc(z_out, 1)

            for n in range(NU + 4):
                if n < NU:
                    softplus(n)
                if n >= 4 and units[n - 4]["last"]:
                    chain_out(n - 4)

            e.wait_ge(z_later, NU)

            def residual(i):
                e.wait_ge(xr_in[i % 2], 16 * (i // 2 + 1))
                if i >= 2:
                    e.wait_ge(e_norm, i - 1)
                    e.wait_ge(e_st[i % 2], 32 * (i // 2))
                for nh in range(2):
                    g = 2 * i + nh
                    e.wait_ge(e_prj, g + 1)
                    e.tensor_tensor(x2[:, i % 2, nh * CH:(nh + 1) * CH], bank[g % 4][:, :],
                                    x_re[:, i % 2, nh * CH:(nh + 1) * CH], ALU.add).then_inc(e_x2, 1)
                e.wait_ge(e_sq, i + 1)
                e.tensor_scalar(ms2[:, i:i + 1], ssq2[:, i:i + 1], 1.0 / D, EPS, ALU.mult, ALU.add).then_inc(e_ms, 1)
                e.wait_ge(e_root, i + 1)
                e.reciprocal(rstd2[:, i:i + 1], ms2[:, i:i + 1]).then_inc(e_inv, 1)

            def scaled(i):
                for hf in range(2):
                    e.wait_ge(e_tr, 2 * i + hf + 1)
                    if i >= 2:
                        e.wait_ge(e_log, i - 1)
                    g = vecs[:, V_FG + 4 * hf:V_FG + 4 * hf + 4]
                    e.tensor_tensor(xfT[:, i % 2, 4 * hf:4 * hf + 4, :],
                                    bank[4 + hf][:, :].rearrange("p (k t) -> p k t", t=P),
                                    g.unsqueeze(2).to_broadcast([P, 4, P]), ALU.mult).then_inc(e_xf, 1)

            def best(i):
                e.wait_ge(e_log, i + 1)
                e.tensor_tensor(logits[:, i, :], bank[6][:, 0:NE], brt, ALU.add).then_inc(e_logb, 1)
                e.wait_ge(e_logb, 3 * i + 1)
                e.max(top_v[:, i, :], logits[:, i, :]).then_inc(e_logb, 1)
                e.wait_ge(e_logb, 3 * i + 2)
                e.max_index(top_i[:, i, :].bitcast(U32), top_v[:, i, :], logits[:, i, :]).then_inc(e_logb, 1)

            e.wait_ge(rt_in, 32)
            for i in range(NT + 2):
                if i < NT:
                    residual(i)
                if 1 <= i <= NT:
                    scaled(i - 1)
                if 2 <= i:
                    best(i - 2)

            count = [0]

            def step(ins):
                count[0] += 1
                ins.then_inc(f_step, 1)
                e.wait_ge(f_step, count[0])

            wide = [P, NT, 4, NE]
            e.wait_ge(e_logb, 24)
            step(e.tensor_tensor(f_w, top_v[:, :, 0:4], top_v[:, :, 0:1].to_broadcast([P, NT, 4]), ALU.subtract))
            step(e.tensor_copy(f_i, top_i.bitcast(U32)))
            step(e.tensor_tensor(f_a, f_i[:, :, 0:4].unsqueeze(3).to_broadcast(wide),
                                 iota_e.unsqueeze(1).unsqueeze(1).to_broadcast(wide), ALU.is_equal))
            step(e.tensor_reduce(f_m, f_a.rearrange("p i k e -> p i e k"), X, ALU.add))
            e.wait_ge(f_exp, 1)
            step(e.tensor_reduce(f_s, f_w, X, ALU.add))
            step(e.reciprocal(f_s, f_s))
            step(e.tensor_tensor(f_w, f_w, f_s.unsqueeze(2).to_broadcast([P, NT, 4]), ALU.mult))
            step(e.tensor_tensor(f_b, f_a, f_w.unsqueeze(3).to_broadcast(wide), ALU.mult))
            three = [P, NT, NE]
            step(e.tensor_reduce(f_t, f_b.rearrange("p i k e -> p i e k"), X, ALU.add))
            step(e.tensor_copy(twx[:, :, 0:NE, 0], f_t))
            step(e.tensor_tensor(f_t, f_t, twx[:, :, 0:NE, 0], ALU.subtract))
            step(e.tensor_copy(twx[:, :, 0:NE, 1], f_t))
            step(e.tensor_tensor(f_t, f_t, twx[:, :, 0:NE, 1], ALU.subtract))
            step(e.tensor_copy(twx[:, :, 0:NE, 2], f_t))
            step(e.memset(twx[:, :, NE, :], 0.0))
            e.wait_ge(f_rank, 1)
            step(e.tensor_copy(f_r, bank[2][:, 0:NT * NE].rearrange("p (i e) -> p i e", e=NE)))
            step(e.tensor_tensor(f_c, bank[3][:, 0:NE].unsqueeze(1).to_broadcast(three),
                                 tok_id.unsqueeze(2).to_broadcast(three), ALU.add))
            step(e.scalar_tensor_tensor(f_c, f_r, -2.0, f_c, ALU.mult, ALU.add))
            step(e.tensor_scalar(f_m, f_m, -1.0, 1.0, ALU.mult, ALU.add))
            step(e.tensor_tensor(f_c, f_c, f_m, ALU.mult))
            step(e.tensor_tensor(pos[:, :, 0:NE], f_r, f_c, ALU.add))
            step(e.tensor_copy(pos[:, :, NE:NE + 1], tok_id.unsqueeze(2)))

            def list_hot(n, x_e):
                e.tensor_scalar(pos_s, pos[:, :, bass.ds(x_e, 1)].rearrange("p i o -> p (i o)"), it_base[:, bass.ds(n, 1)],
                                None, ALU.subtract).then_inc(l_pos, 1)
                e.scalar_tensor_tensor(tw_s[:, :, 2:5], pos[:, :, bass.ds(x_e, 1)].to_broadcast([P, NT, 3]),
                                       it_low[:, bass.ds(n, 1)],
                                       twx[:, :, bass.ds(x_e, 1), :].rearrange("p i o c -> p i (o c)"), ALU.is_ge, ALU.mult)
                e.wait_ge(l_pos, n + 1)
                e.tensor_tensor(hot, pos_s.unsqueeze(2).to_broadcast([P, NT, CAP]),
                                iota_cap.unsqueeze(1).to_broadcast([P, NT, CAP]), ALU.is_equal).then_inc(l_hot, 1)

            def list_out(n):
                sums = bank[7][0:HC, 0:10].rearrange("p (h c) -> p h c", c=5)
                e.tensor_reduce(l_raw, sums[:, :, 0:2], X, ALU.add).then_inc(l_id, 1)
                e.tensor_reduce(wsel, sums[:, :, 2:5], X, ALU.add)
                e.wait_ge(l_id, n + 1)
                e.tensor_copy(idx, l_raw).then_inc(l_ok, 1)

            def tokens_out(m):
                n = 3 if m < 2 else 2
                g = vecs[:, V_FG + 3 * m:V_FG + 3 * m + n]
                e.tensor_tensor(xT[:, 3 * m:3 * m + n, :], bank[4 + m][:, 0:n * CAP].rearrange("p (k t) -> p k t", t=CAP),
                                g.unsqueeze(2).to_broadcast([P, n, CAP]), ALU.mult).then_inc(g_xT, 1)

            built = [0]

            def table(ins):
                built[0] += 1
                ins.then_inc(it_step, 1)
                e.wait_ge(it_step, built[0])

            e.tensor_copy(f_cnt, bank[3][:, 0:NE])
            e.tensor_copy(tw_s[:, :, 0], tile_at)
            e.tensor_copy(tw_s[:, :, 1], tok_id[:, 0:1].to_broadcast([P, NT]))
            e.memset(it_base, 0.0)
            e.memset(it_low, 0.0)
            table(e.tensor_copy(it_i[:, 1, 0:NE], bank[3][:, 0:NE]))
            list_hot(0, 0)
            e.wait_ge(l_sum, 1)
            list_out(0)
            e.wait_ge(l_ok, 1)
            e.tensor_copy(idx_sc, idx)
            e.memset(w_sc, 0.0)
            e.memset(yT, 0.0).then_inc(m_y, 2)
            e.wait_ge(bias_tr, 1)
            for m in range(2):
                e.tensor_copy(btab[:, :, 12 * m:12 * m + 12],
                              bank[m][:, 0:12 * NE].rearrange("p (j e) -> p e j", e=NE)).then_inc(bias_ok, 1)
            e.wait_ge(bias_ok, 2)
            e.tensor_scalar(btab[:, :, 8:16], btab[:, :, 8:16], 1.0, None, ALU.add).then_inc(bias_ok, 1)
            e.wait_ge(bias_ok, 3)
            for m in range(3):
                e.wait_ge(g_tr, m + 1)
                tokens_out(m)
            grid = [P, NX, NE]
            few = region(work, 0, NE, NB1)
            table(e.tensor_tensor(few, f_cnt.unsqueeze(2).to_broadcast([P, NE, NB1]),
                                  further.unsqueeze(1).to_broadcast([P, NE, NB1]), ALU.is_gt))
            table(e.tensor_reduce(f_over, few, X, ALU.add))
            table(e.tensor_tensor_scan(f_cum, ones[:, 0:NE], f_over, 0.0, ALU.mult, ALU.add))
            table(e.tensor_tensor(f_x, f_cum.unsqueeze(1).to_broadcast(grid), iota_x.unsqueeze(2).to_broadcast(grid),
                                  ALU.is_le))
            table(e.tensor_reduce(it_f[:, 0, NE:NI], f_x, X, ALU.add))
            table(e.tensor_tensor(f_y, f_x, f_over.unsqueeze(1).to_broadcast(grid), ALU.mult))
            table(e.tensor_reduce(f_prior, f_y, X, ALU.add))
            table(e.tensor_tensor(f_prior, iota_x, f_prior, ALU.subtract))
            table(e.tensor_scalar(it_low[:, NE:NI], f_prior, float(CAP), float(CAP), ALU.mult, ALU.add))
            table(e.tensor_scalar(it_base[:, NE:NI], it_low[:, NE:NI], float(S - CAP), None, ALU.min))
            table(e.tensor_tensor(f_x, it_f[:, 0, NE:NI].unsqueeze(2).to_broadcast(grid),
                                  iota_e.unsqueeze(1).to_broadcast(grid), ALU.is_equal))
            table(e.tensor_tensor(f_y, f_x, f_cnt.unsqueeze(1).to_broadcast(grid), ALU.mult))
            table(e.tensor_reduce(f_prior, f_y, X, ALU.add))
            table(e.tensor_tensor(it_f[:, 1, NE:NI], f_prior, it_base[:, NE:NI], ALU.subtract))
            table(e.tensor_copy(it_f[:, 1, NI - 1:NI], f_cum[:, NE - 1:NE]))
            table(e.tensor_copy(it_f[:, 0, 0:NE], iota_e))
            e.tensor_copy(it_i[:, 0, :], it_f[:, 0, :])
            table(e.tensor_copy(it_i[:, 1, NE:NI], it_f[:, 1, NE:NI]))
            assert built[0] == IT_STEPS
            for s_ in (m_up, m_gs, m_hid):
                e.sem_inc(s_, 2)

            def block_dve(n, x_e):
                e.wait_ge(m_y, n * 8 + 2)
                e.tensor_copy(be, btab[:, bass.ds(x_e, 1), :].rearrange("p o j -> p (o j)")).then_inc(m_bias, 1)
                e.wait_ge(m_bias, n + 1)
                for f in range(KD):
                    b = f % 2
                    e.wait_ge(m_gu, n * 8 + (f + 1))
                    e.wait_ge(m_hid, n * 8 + (f + 1))
                    e.tensor_scalar(g1[:, b], bank[b][:, 0:CAP], be[:, f:f + 1], GLIM, ALU.add, ALU.min)\
                        .then_inc(m_gate, 1)
                    e.tensor_scalar(u1[:, b], bank[b][:, CAP:2 * CAP], be[:, 8 + f:9 + f], GLIM + 1.0,
                                    ALU.add, ALU.min).then_inc(m_up, 1)
                    e.wait_ge(m_sig, n * 8 + (f + 1))
                    e.wait_ge(m_up, n * 8 + (f + 3))
                    e.tensor_tensor(gs[:, b], g1[:, b], sg[:, b], ALU.mult).then_inc(m_gs, 1)
                    e.wait_ge(m_gs, n * 8 + (f + 3))
                    e.scalar_tensor_tensor(hid[:, f, :], u1[:, b], 1.0 - GLIM, gs[:, b], ALU.max, ALU.mult)\
                        .then_inc(m_hid, 1)
                    if f == 2:
                        e.wait_ge(l_sum, n + 1)
                        list_hot(n + 1, e.value_load(it_i[0:1, 0, bass.ds(n + 1, 1)], min_val=0, max_val=NE))
                    if f == 6:
                        e.wait_ge(l_ok, n + 1)
                        e.wait_ge(m_yo, n * 4 + 4)
                        e.wait_ge(sc_done, n * 32 + 48)
                        e.tensor_copy(idx_sc, idx)
                        e.tensor_copy(w_sc, wsel).then_inc(l_keep, 1)
                        e.wait_ge(l_keep, n + 1)
                        e.wait_ge(l_sum, n + 2)
                        list_out(n + 1)
                e.wait_ge(m_ytr, n * 4 + 4)
                for j in range(KD):
                    e.wait_ge(m_dn, n * 8 + (j + 1))
                    e.tensor_scalar(yT[:, j, :], bank[2 + j % 2][:, 0:CAP], be[:, 16 + j:17 + j], None, ALU.add)\
                        .then_inc(m_y, 1)
                    if j == 6:
                        for m in range(3):
                            e.wait_ge(g_tr, n * 3 + (m + 4))
                            tokens_out(m)

            with e.Fori(0, NE) as n:
                block_dve(n, n)
            more = e.value_load(it_i[0:1, 1, NI - 1:NI], min_val=0, max_val=NX - 1)
            with e.If(more > 0):
                with e.Fori(NE, more + NE) as n:
                    block_dve(n, e.value_load(it_i[0:1, 0, bass.ds(n, 1)], min_val=0, max_val=NE - 1))


_INS = ["x", "attn_norm_g", "w_in", "ret_norm_g", "sb_q_norm_g", "sb_k_norm_g", "w_out", "ffn_norm_g",
        "w_router", "b_router", "w_gate_up", "b_gate_up", "w_down", "b_down"]


def kernel(**inputs):
    import concourse.bacc as bacc
    from concourse.bass_utils import run_bass_kernel_spmd

    nc = bacc.Bacc("TRN2", target_bir_lowering=False, num_devices=1)
    arrays = {f"in_{name}": np.ascontiguousarray(inputs[name]) for name in _INS}
    arrays["in_consts"], arrays["in_rope"] = constants()
    args = [nc.dram_tensor(n, a.shape, mybir.dt.from_np(a.dtype), kind="ExternalInput").ap() for n, a in arrays.items()]
    args.append(nc.dram_tensor("out_x", (1, S, D), F32, kind="ExternalOutput").ap())
    layer(nc, *args)
    r = run_bass_kernel_spmd(nc, [arrays], core_ids=[0])
    return r.results[0]["out_x"]
```

```python
from contextlib import ExitStack

import numpy as np
import concourse.bass as bass
from concourse import mybir

F32 = mybir.dt.float32
U32 = mybir.dt.uint32
I32 = mybir.dt.int32
BF16 = mybir.dt.bfloat16
F32R = mybir.dt.float32r
ALU = mybir.AluOpType
ACT = mybir.ActivationFunctionType
X = mybir.AxisListType.X

P = 128
S = 1024
D = 1024
NT = S // P
KD = D // P
RH = 4
SH = 8
HD = 64
NIN = 3584
CH = 512
SL = 256
HT = NT // 2
NE = 32
CAP = 168
HC = CAP // 2
TOPK = 4
NB1 = -(-S // CAP) - 1
NX = TOPK * S // CAP + 1
NI = NE + NX
WIDTHS = (*range(128, CAP, 4), CAP)
IT_STEPS = 18
EPS = 1e-6
BIG = 1.0e30
GLIM = 7.0
GALPHA = 1.702

C_ID, C_NU, C_NO, C_MB, C_BO, C_LS, C_ON, C_CA = (P * i for i in range(8))
C_IO = 8 * P
C_I32 = C_IO + CAP
C_TID = C_I32 + NE
C_TIL = C_TID + NT
C_GV = C_TIL + NT
C_GO = C_GV + NT * RH
C_TH = C_GO + NT * RH
C_IX = C_TH + NB1
C_N = C_IX + NX
V_AG, V_FG, V_RG, V_SQ, V_SK, V_N = 0, 8, 16, 20, 21, 22


def constants():
    t = np.zeros((P, C_N), np.float32)
    r, c = np.arange(P)[:, None], np.arange(P)[None, :]
    t[:, C_ID:C_ID + P] = r == c
    t[:, C_NU:C_NU + P] = np.where(r >= c, -1.0, 0.0)
    t[:, C_NO:C_NO + P] = -1.0
    t[:, C_MB:C_MB + P] = np.where(r >= c, -BIG, 0.0)
    t[:, C_BO:C_BO + P] = (r // HD) == (c // HD)
    t[:, C_LS:C_LS + P] = r < c
    t[:, C_ON:C_ON + P] = 1.0
    t[:, C_CA:C_CA + P] = r <= c
    t[:, C_IO:C_IO + CAP] = np.arange(CAP)
    t[:, C_I32:C_I32 + NE] = np.arange(NE)
    tok = np.arange(NT)[None, :] * P + np.arange(P)[:, None]
    t[:, C_TID:C_TID + NT] = tok
    t[:, C_TIL:C_TIL + NT] = np.arange(NT) * P
    gamma = 1.0 - 2.0 ** (-5.0 - np.arange(RH, dtype=np.float64))
    g = np.log(gamma)[None, None, :]
    t[:, C_GV:C_GV + NT * RH] = np.exp(-(tok[:, :, None] + 1) * g).reshape(P, -1)
    t[:, C_GO:C_GO + NT * RH] = (np.exp((tok[:, :, None] + 1) * g) * P ** -0.5).reshape(P, -1)
    t[:, C_TH:C_TH + NB1] = CAP * (1 + np.arange(NB1))
    t[:, C_IX:C_IX + NX] = np.arange(NX)
    half = P // 2
    inv = (np.float32(10000.0) ** (-np.arange(half, dtype=np.float32) / np.float32(half))).astype(np.float32)
    ang = np.arange(S, dtype=np.float32)[None, :] * inv[:, None]
    cos, sin = np.cos(ang), np.sin(ang)
    rope = np.concatenate([np.concatenate([cos, cos]), np.concatenate([sin, -sin])], axis=1)
    return t, rope.astype(np.float32)


def layer(nc, x, attn_norm_g, w_in, ret_norm_g, sb_q_norm_g, sb_k_norm_g, w_out, ffn_norm_g,
          w_router, b_router, w_gate_up, b_gate_up, w_down, b_down, consts, rope, out):
    with ExitStack() as ctx:
        ctx.enter_context(nc.allow_non_contiguous_dma(reason="small vectors"))
        ctx.enter_context(nc.allow_low_precision(reason="sums of zeros and ones, exact in bfloat16"))

        def sb(name, shape, dt=F32):
            return ctx.enter_context(nc.sbuf_tensor(name, shape, dt))

        def sem(name):
            return ctx.enter_context(nc.semaphore(name))

        with nc.sbuf_tensor("ring_r", [P, 24576], F32R) as ring_r, nc.sbuf_tensor("hx_r", [P, 8192], F32R) as hx_r, \
                nc.sbuf_tensor("mix_r", [P, 8192], F32R) as mix_r, nc.sbuf_tensor("work_r", [P, 9728], F32R) as work_r:
            pass
        ring = sb("ring", [P, 24576])
        hx = sb("hx", [P, 8192])
        mix = sb("mix", [P, 8192])
        work = sb("work", [P, 9728])
        cst = sb("cst", [P, C_N])
        small = sb("small", [P, 1154])
        bank = [ctx.enter_context(nc.psum_tensor(f"bank{i}", [P, 512], F32)) for i in range(8)]
        xn_dram = nc.dram_tensor("xn_scratch", [S, D], F32, kind="Internal").ap()

        ident = cst[:, C_ID:C_ID + P]
        neg_upper = cst[:, C_NU:C_NU + P]
        neg_ones = cst[:, C_NO:C_NO + P]
        mask_bias = cst[:, C_MB:C_MB + P]
        block_ones = cst[:, C_BO:C_BO + P]
        before = cst[:, C_LS:C_LS + P]
        ones = cst[:, C_ON:C_ON + P]
        causal = cst[:, C_CA:C_CA + P]
        iota_cap = cst[:, C_IO:C_IO + CAP]
        iota_e = cst[:, C_I32:C_I32 + NE]
        tok_id = cst[:, C_TID:C_TID + NT]
        tile_at = cst[:, C_TIL:C_TIL + NT]
        g_v = cst[:, C_GV:C_GV + NT * RH].rearrange("p (i h) -> p i h", h=RH)
        further = cst[:, C_TH:C_TH + NB1]
        iota_x = cst[:, C_IX:C_IX + NX]
        g_o = cst[:, C_GO:C_GO + NT * RH].rearrange("p (i h) -> p i h", h=RH)

        def region(t, at, *shape):
            n = int(np.prod(shape))
            v = t[:, at:at + n]
            if len(shape) == 1:
                return v
            names = "abcd"[:len(shape)]
            return v.rearrange(f"p ({' '.join(names)}) -> p {' '.join(names)}",
                               **{k: s for k, s in zip(names, shape)})

        rqT = region(ring, 0, RH, CH)
        rkT = region(ring, 2048, RH, CH)
        rv = region(ring, 4096, HT, CH)
        rope_t = region(ring, 6144, 2, CH)
        x_raw = region(ring, 8192, KD, CH)
        sqT = region(ring, 12288, 4, S)
        skT = region(ring, 16384, 4, S)
        sv = region(ring, 20480, NT, CH)
        x_in = [region(ring, 12288 + 1024 * i, D) for i in range(HT)]
        square_dump = region(ring, 16384, D)
        x_norm = [region(ring, 20480 + 1024 * i, D) for i in range(2)]
        x_hi = region(hx_r, 0, KD, CH)
        x_lo = region(hx_r, 4096, KD, CH)
        wo = region(hx, 0, KD, D)
        wo_hi, wo_lo = region(ring_r, 8192, KD, D), region(hx_r, 0, KD, D)
        mix_hi, mix_lo = region(ring_r, 0, KD, S), region(mix_r, 0, KD, S)
        mixT = region(mix, 0, KD, S)
        w_raw = [region(mix, 4096, KD, SL), region(work, 0, KD, SL)]
        w_hi = [region(mix_r, 6144, KD, SL), region(work_r, 2048, KD, SL)]
        w_lo = [region(mix_r, 4096, KD, SL), region(work_r, 0, KD, SL)]
        k_tok = region(work, 4096, 2, CH)
        s_msk = region(work, 5120, 2, CH)
        state = region(work, 6144, CH)
        o_buf = region(work, 6656, 2, CH)
        o_sq = region(work, 7680, CH)
        prj_tmp = region(work, 8192, 2, CH)
        prj_std = region(work, 9216, CH)
        soft = region(work, 0, 3, CH)
        sp = region(work, 1536, 3, CH)
        wgt = region(work, 3072, 3, CH)
        sp_hi = region(work_r, 4608, 3, CH)
        sp_lo = region(work_r, 6144, 3, CH)
        neg_upper_r = region(ring_r, 0, P)
        ident_r = region(ring_r, 128, P)
        mask_r = region(ring_r, 256, P)
        k_st = [region(ring_r, at, 2, S) for at in (7168, 1024)]
        q_st = [region(ring_r, at + 2 * S, 2, S) for at in (7168, 1024)]
        q_low = [region(ring_r, at + 4 * S, S) for at in (7168, 1024)]
        later = region(work, 7680, 2, 2, CH)
        x_re = region(work, 0, 2, D)
        x2 = region(work, 2048, 2, D)
        xn2 = region(work, 4096, 2, D)
        xfT = region(work, 6144, 2, KD, P)
        e_dump = region(work, 8192, D)
        vec_rows = small[0:V_N, 0:P]
        vecs = small[:, 128:128 + V_N]
        sbq_g = small[:, 150:151]
        ssq = small[:, 152:160]
        ms = small[:, 160:168]
        rstd = small[:, 168:176]
        ret_ss = small[:, 176:192].rearrange("p (b h) -> p b h", h=RH)
        brt = small[:, 192:224]
        eps = small[:, 888:889]
        logits = region(small, 224, NT, NE)
        top_v = region(small, 480, NT, 8)
        top_i = region(small, 544, NT, 8)
        wr = region(small, 608, KD, NE)
        f_i = small[:, 890:898]
        f_m = region(small[:, 898:1026].bitcast(BF16), 0, NT, NE)
        before_b = small[:, 1026:1090].bitcast(BF16)
        ones_b = small[:, 1090:1154].bitcast(BF16)
        ssq2, ms2, rstd2 = small[:, 864:872], small[:, 872:880], small[:, 880:888]

        const_in = sem("const_in")
        rope_in = sem("rope_in")
        vec_in = sem("vec_in")
        xt_in = [sem(f"xt_in{i}") for i in range(HT)]
        win_in = [sem(f"win_in{i}") for i in range(2)]
        vec_tr = sem("vec_tr")
        vec_ok = sem("vec_ok")
        a_sq = sem("a_sq")
        a_ms = sem("a_ms")
        a_root = sem("a_root")
        a_inv = sem("a_inv")
        a_norm = sem("a_norm")
        a_tr = sem("a_tr")
        a_hx = sem("a_hx")
        xs_hi = sem("xs_hi")
        xs_lo = sem("xs_lo")
        ws_hi = sem("ws_hi")
        ws_lo = sem("ws_lo")
        prj = sem("prj")
        prj_free = sem("prj_free")
        rope_ok = sem("rope_ok")
        gate_sig = sem("gate_sig")
        qk_sq = sem("qk_sq")
        qk_sum = sem("qk_sum")
        eps_ok = sem("eps_ok")
        qk_ln = sem("qk_ln")
        qk_inv = sem("qk_inv")
        r_score = sem("r_score")
        r_ktr = sem("r_ktr")
        r_mask = sem("r_mask")
        r_k = sem("r_k")
        r_out = sem("r_out")
        r_acc = sem("r_acc")
        r_state = sem("r_state")
        r_o = sem("r_o")
        r_osq = sem("r_osq")
        r_ms = sem("r_ms")
        r_ln = sem("r_ln")
        r_inv = sem("r_inv")
        r_norm = sem("r_norm")
        r_tr = sem("r_tr")
        r_mix = sem("r_mix")
        wo_in = sem("wo_in")
        z_st = sem("z_st")
        z_ok = sem("z_ok")
        z_abs = sem("z_abs")
        z_exp = sem("z_exp")
        z_ln = sem("z_ln")
        z_sp = sem("z_sp")
        z_const = sem("z_const")
        z_hi = sem("z_hi")
        z_lo = sem("z_lo")
        z_zero = sem("z_zero")
        z_later = sem("z_later")
        z_cum = sem("z_cum")
        z_w = sem("z_w")
        z_pv = sem("z_pv")
        z_out = sem("z_out")
        xr_in = [sem(f"xr_in{i}") for i in range(2)]
        rt_in = sem("rt_in")
        es_hi = sem("es_hi")
        es_lo = sem("es_lo")
        e_prj = sem("e_prj")
        e_x2 = sem("e_x2")
        e_sq = sem("e_sq")
        e_ms = sem("e_ms")
        e_root = sem("e_root")
        e_inv = sem("e_inv")
        e_norm = sem("e_norm")
        e_st = [sem(f"e_st{i}") for i in range(2)]
        e_tr = sem("e_tr")
        e_xf = sem("e_xf")
        e_log = sem("e_log")
        e_logb = sem("e_logb")
        b_ok = sem("b_ok")
        f_step = sem("f_step")
        f_exp = sem("f_exp")
        f_rank = sem("f_rank")
        it_step = sem("it_step")
        l_pos = sem("l_pos")
        pool_go = sem("pool_go")
        bias_in = sem("bias_in")
        bias_tr = sem("bias_tr")
        bias_ok = sem("bias_ok")
        gu_in = [sem(f"gu_in{c}") for c in range(4)]
        dn_in = [sem(f"dn_in{c}") for c in range(2)]
        l_hot = sem("l_hot")
        l_id = sem("l_id")
        l_sum = sem("l_sum")
        l_keep = sem("l_keep")
        l_ok = sem("l_ok")
        g_in = sem("g_in")
        g_tr = sem("g_tr")
        g_xT = sem("g_xT")
        m_bias = sem("m_bias")
        m_gu = sem("m_gu")
        m_gate = sem("m_gate")
        m_up = sem("m_up")
        m_sig = sem("m_sig")
        m_gs = sem("m_gs")
        m_hid = sem("m_hid")
        m_dn = sem("m_dn")
        m_y = sem("m_y")
        m_ytr = sem("m_ytr")
        m_yo = sem("m_yo")
        sc_done = sem("sc_done")

        block = ctx.enter_context(nc.Block())

        T_CHUNKS = (0, 1, 3, 4, 5)
        NSLAB = 2 * 7 * CH // SL
        groups = []
        for slab in range(NSLAB):
            th, c = slab // (NSLAB // 2), slab % (NSLAB // 2) // 2
            for s in range(2 if c in T_CHUNKS else HT):
                groups.append(dict(th=th, c=c, slab=slab, s=s, row=2 * (slab % 2) + s))
        NG = len(groups)
        end_of = {u["slab"]: g + 1 for g, u in enumerate(groups)}
        SPLIT = {g: u["slab"] + 1 for g, u in enumerate(groups)
                 if u["slab"] + 1 < NSLAB and u["s"] == (0 if u["c"] in T_CHUNKS else 1)}
        QK = [g for g, u in enumerate(groups) if u["c"] in (4, 5)]
        NORM = {g: HT + g for g in range(HT)}
        TURN = {g + 1: HT + g for g in range(HT)}
        RSTEP = {NG // 2 * th + g: (th, t) for th in range(2) for t, g in enumerate((21, 23, 25, 27, 30, 33))}

        def chunk_at(th, t):
            return HT * th + t if 0 <= t < HT else None

        streams = [[], []]
        for h in range(SH):
            for th in ((1, 0), (0, 1))[h % 2]:
                top = 4 * th + 3
                for b in range(top, -1, -1):
                    t0 = max(b * P, th * CH)
                    streams[h % 2].append(dict(h=h, th=th, b=b, par=h % 2, t0=t0, o0=t0 - th * CH,
                                               diag=b * P >= th * CH, first=b == top, last=b == 0,
                                               step=top - b, chain=2 * (h // 2) + (th == h % 2)))
        units = [u for two in zip(*streams) for u in two]

        def of_chain(par, chain, end):
            return next(n for n, u in enumerate(units) if (u["par"], u["chain"]) == (par, chain) and u[end])

        def nth(n, end):
            return sum(u[end] for u in units[:n + 1])

        def out_bank(u):
            return bank[4 + u["par"] + 2 * (u["chain"] % 2)]

        NU = len(units)

        def split_parts():
            def tile(i, k):
                at = (slice(None), slice(k, k + 4), slice(i * P, (i + 1) * P))
                return mixT[at], mix_hi[at], mix_lo[at]

            yield tile(0, 0)
            for nh in range(2):
                for k in range(KD):
                    at = (slice(None), k, slice(nh * CH, (nh + 1) * CH))
                    yield wo[at], wo_hi[at], wo_lo[at]
                    if nh == 0 and k == 0:
                        yield tile(0, 4)
            for i in range(1, NT):
                for k in (0, 4):
                    yield tile(i, k)

        PAIR = NU // (SH // 2)

        hid = region(hx, 0, KD, CAP)
        xT = region(hx, 1344, KD, CAP)
        yT = region(hx, 2688, KD, CAP)
        hot = region(hx[:, 4032:4032 + NT * CAP // 2].bitcast(BF16), 0, NT, CAP)
        g1 = region(hx, 5376, 2, CAP)
        u1 = region(hx, 5712, 2, CAP)
        sg = region(hx, 6048, 2, CAP)
        gs = region(hx, 6384, 2, CAP)
        be = region(hx, 6720, 24)
        l_raw = region(hx, 6744, 2)[0:HC]
        idx = hx[0:HC, 6760:6762].bitcast(U32)
        wsel = hx[0:HC, 6762:6764]
        idx_sc = hx[0:HC, 6764:6766].bitcast(U32)
        w_sc = hx[0:HC, 6766:6768]
        btab = region(hx, 6784, NE, 24)
        pos_s = region(hx, 6768, NT)
        tw_s = region(hx[:, 7552:7552 + NT * 5 // 2].bitcast(BF16), 0, NT, 5)
        xg = region(mix, 0, 2, D)[0:HC]
        yo = region(mix, 2048, 2, D)[0:HC]
        pos = region(mix, 4096, NT, NE + 1)
        twx = region(mix[:, 4360:4360 + NT * (NE + 1) * 3 // 2].bitcast(BF16), 0, NT, NE + 1, 3)
        f_a = region(work[:, 9216:9728].bitcast(BF16), 0, NT, 4, NE)
        f_b = region(work, 0, NT, 4, NE)
        f_n = region(work, 8192, NT, NE)
        f_r = region(work, 8448, NT, NE)
        f_c = region(work, 8704, NT, NE)
        f_w = region(work, 8960, NT, 4)
        f_s = region(work, 8992, NT)
        f_t = region(work, 1024, NT, NE)
        f_over = region(work, 9064, NE)
        f_cum = region(work, 9096, NE)
        f_cnt = region(work, 9128, NE)
        f_prior = region(work, 9160, NX)
        f_x = region(work, 0, NX, NE)
        f_y = region(work, 1024, NX, NE)
        it_base = region(mix, 5024, NI)
        it_low = region(mix, 5088, NI)
        it_f = region(mix, 5152, 2, NI)
        it_i = region(mix, 5280, 2, NI).bitcast(I32)
        b_rows = region(work, 4096, 3072)[0:NE]
        gu_ring = region(ring, 0, KD, 2048)
        dn_ring = region(ring, 16384, KD, D)

        xr = x[0].rearrange("(i p) d -> i p d", p=P)
        outr = out[0].rearrange("(i p) d -> i p d", p=P)
        out_rows = out[0]
        xnr = xn_dram.rearrange("(i p) d -> i p d", p=P)
        win_r = w_in[0].rearrange("(k p) (c n) -> c p k n", p=P, n=SL)
        rope_r = rope.rearrange("p (a h n) -> h p a n", a=2, h=2)
        gu_r = w_gate_up[0].rearrange("e (k p) (c n) -> e c p k n", p=P, n=512)
        dn_r = w_down[0].rearrange("e (k p) (c n) -> e c p k n", p=P, n=512)

        @block.sync
        def _(sp_eng):
            e = sp_eng
            def load_vectors():
                e.dma_start(vec_rows[V_AG:V_AG + 8], attn_norm_g[0].rearrange("(k p) -> k p", p=P)).then_inc(vec_in, 16)
                e.dma_start(vec_rows[V_FG:V_FG + 8], ffn_norm_g[0].rearrange("(k p) -> k p", p=P)).then_inc(vec_in, 16)
                e.dma_start(vec_rows[V_RG:V_RG + 4], ret_norm_g[0]).then_inc(vec_in, 16)
                for r, g in ((V_SQ, sb_q_norm_g), (V_SK, sb_k_norm_g)):
                    for h in range(2):
                        e.dma_start(vec_rows[r:r + 1, h * HD:(h + 1) * HD], g).then_inc(vec_in, 16)

            def load_slab(j):
                if j >= 2:
                    e.wait_ge(prj, end_of[j - 2])
                e.dma_start(w_raw[j % 2], win_r[j % (NSLAB // 2)]).then_inc(win_in[j % 2], 16)

            for i in range(NT):
                if i >= HT:
                    e.wait_ge(a_norm, i - HT + 1)
                e.dma_start(x_in[i % HT], xr[i]).then_inc(xt_in[i % HT], 16)
                if i == 1:
                    load_vectors()
                if i == HT - 1:
                    load_slab(0)
                    e.dma_start(rope_t, rope_r[0]).then_inc(rope_in, 16)
                    load_slab(1)
            for j in range(2, NSLAB):
                load_slab(j)
                if j == 8:
                    e.wait_ge(rope_ok, 2 * RH)
                    e.dma_start(rope_t, rope_r[1]).then_inc(rope_in, 16)
            e.wait_ge(prj, NG)
            e.dma_start(wo, w_out[0].rearrange("(k p) n -> p k n", p=P)).then_inc(wo_in, 16)
            e.wait_ge(z_pv, NU)
            for c in range(2):
                e.dma_start(dn_ring[:, :, c * 512:(c + 1) * 512], dn_r[0, c]).then_inc(dn_in[c], 16)
            for i in range(NT):
                e.wait_ge(e_x2, 2 * i + 2)
                e.dma_start(outr[i], x2[:, i % 2]).then_inc(e_st[i % 2], 16)
                e.wait_ge(e_norm, i + 1)
                e.dma_start(xnr[i], xn2[:, i % 2]).then_inc(e_st[i % 2], 16)
            e.wait_ge(e_prj, 2 * NT)
            for c in range(4):
                e.dma_start(gu_ring[:, :, c * 512:(c + 1) * 512], gu_r[0, c]).then_inc(gu_in[c], 16)

            def load_expert(n, x_e):
                for c in range(4):
                    e.wait_ge(m_gu, n * 8 + (2 * c - 6))
                    e.dma_start(gu_ring[:, :, c * 512:(c + 1) * 512], gu_r[x_e, c]).then_inc(gu_in[c], 16)
                for c in range(2):
                    e.wait_ge(m_dn, n * 8 + (4 * c - 4))
                    e.dma_start(dn_ring[:, :, c * 512:(c + 1) * 512], dn_r[x_e, c]).then_inc(dn_in[c], 16)

            with e.Fori(1, NE) as n:
                load_expert(n, n)
            e.wait_ge(it_step, IT_STEPS)
            more = e.value_load(it_i[0:1, 1, NI - 1:NI], min_val=0, max_val=NX - 1)
            with e.If(more > 0):
                with e.Fori(NE, more + NE) as n:
                    load_expert(n, e.value_load(it_i[0:1, 0, bass.ds(n, 1)], min_val=0, max_val=NE - 1))

        @block.gpsimd
        def _(e):
            e.dma_start(brt, b_router.to_broadcast([P, NE])).then_inc(rt_in, 16)
            e.dma_start(wr, w_router[0].rearrange("(k p) n -> p k n", p=P)).then_inc(rt_in, 16)
            for th in range(2):
                for q in range(2 * RH):
                    dst = (rqT if q < RH else rkT)[:, q % RH, :]
                    e.wait_ge(prj_free, NG // 2 * th + q + 1)
                    e.tensor_tensor(dst, dst, prj_tmp[:, q % 2], ALU.add).then_inc(rope_ok, 1)
                for c in range(HT * th, HT * (th + 1)):
                    e.wait_ge(r_inv, c + 1)
                    ob = o_buf[:, c % 2].rearrange("p (h n) -> p h n", h=RH)
                    rs = ret_ss[:, 2 + c % 2, :]
                    e.tensor_tensor(ob, ob, rs.unsqueeze(2).to_broadcast([P, RH, P]), ALU.mult).then_inc(r_norm, 1)
            e.wait_ge(r_mix, NT)
            e.wait_ge(prj_free, NG)
            for n, u in enumerate(units):
                lt = later[:, u["par"]]
                rng = slice(u["o0"], CH)
                if u["first"]:
                    if u["chain"]:
                        last = of_chain(u["par"], u["chain"] - 1, "last")
                        e.wait_ge(z_cum, last + 1)
                        e.wait_ge(z_later, last + 1)
                    e.memset(lt, 0.0).then_inc(z_zero, 1)
                    e.wait_ge(z_zero, nth(n, "first"))
                elif n >= 2:
                    e.wait_ge(z_later, n - 1)
                    e.wait_ge(z_cum, n - 1)
                e.wait_ge(z_sp, n + 1)
                k = u["step"]
                e.tensor_tensor(lt[:, (k + 1) % 2, rng], lt[:, k % 2, rng], sp[:, n % 3, rng], ALU.add)\
                    .then_inc(z_later, 1)

            def gather():
                for h in range(2):
                    e.indirect_dma_start(out=xg[:, h], out_offset=None, in_=xn_dram,
                                         in_offset=bass.IndirectOffsetOnAxis(ap=idx[:, h:h + 1], axis=0)).then_inc(g_in, 16)

            e.wait_ge(e_log, NT)
            e.wait_ge(e_st[0], 128)
            e.wait_ge(e_st[1], 128)
            e.dma_start(b_rows[:, 2048:3072], b_down[0]).then_inc(sc_done, 16)
            e.wait_ge(l_ok, 1)
            e.wait_ge(e_st[0], 128)
            e.wait_ge(e_st[1], 128)
            e.wait_ge(e_prj, 16)
            gather()

            def add_rows(n):
                e.wait_ge(sc_done, n * 32 + 16)
                e.wait_ge(m_yo, n * 4 + 4)
                e.sem_inc(pool_go, 1)
                for h in range(2):
                    e.indirect_dma_start(out=out_rows, in_=yo[:, h], in_offset=None, compute_op=ALU.add,
                                         out_offset=bass.IndirectOffsetOnAxis(ap=idx_sc[:, h:h + 1], axis=0)).then_inc(sc_done, 16)

            def block_dmas(n):
                add_rows(n)
                e.wait_ge(l_ok, n + 2)
                e.wait_ge(g_tr, n * 3 + 3)
                e.sem_inc(pool_go, 1)
                gather()

            with e.Fori(0, NE) as n:
                block_dmas(n)
            e.wait_ge(sc_done, 32 * NE + 16)
            e.wait_ge(g_in, 32 * (NE + 1))
            e.wait_ge(it_step, IT_STEPS)
            more = e.value_load(it_i[0:1, 1, NI - 1:NI], min_val=0, max_val=NX - 1)
            with e.If(more > 0):
                with e.Fori(NE, more + NE) as n:
                    block_dmas(n)
                    e.wait_ge(sc_done, n * 32 + 48)
                    e.wait_ge(g_in, n * 32 + 64)
                    e.sem_inc(pool_go, 1)
            add_rows(more + NE)
            e.wait_ge(sc_done, more * 32 + (NE * 32 + 48))

        @block.scalar
        def _(e):
            e.dma_start(cst[:, :], consts).then_inc(const_in, 16)
            def square(i):
                e.wait_ge(xt_in[i % HT], 16 * (i // HT + 1))
                if i:
                    e.wait_ge(a_sq, i)
                e.activation(square_dump, x_in[i % HT], ACT.Square, accum_out=ssq[:, i:i + 1]).then_inc(a_sq, 1)
                e.wait_ge(a_ms, i + 1)
                e.activation(ms[:, i:i + 1], ms[:, i:i + 1], ACT.Sqrt).then_inc(a_root, 1)

            def upper_slab(j):
                e.wait_ge(win_in[j % 2], 16 * (j // 2 + 1))
                e.activation(w_hi[j % 2], w_raw[j % 2], ACT.Copy).then_inc(ws_hi, 1)

            def upper_tokens(th):
                e.wait_ge(a_hx, NT * (th + 1))
                if th:
                    e.wait_ge(prj, NG // 2)
                for k in range(0, KD, 2):
                    e.activation(x_hi[:, k:k + 2], x_raw[:, k:k + 2], ACT.Copy).then_inc(xs_hi, 1)

            for i in range(HT):
                square(i)
            upper_slab(0)
            upper_tokens(0)
            for g, u in enumerate(groups):
                th, c = u["th"], u["c"]
                if g == NG // 2:
                    upper_tokens(1)
                if c == 3:
                    e.wait_ge(prj, g + 1)
                    if u["row"] >= 2:
                        e.wait_ge(prj_free, g - 1)
                    else:
                        e.wait_ge(rope_ok, 2 * RH * (th + 1))
                    e.activation(prj_tmp[:, g % 2], bank[g % 3][:, :], ACT.Sigmoid).then_inc(gate_sig, 1)
                if g in QK:
                    q = QK.index(g)
                    if q % 8 == 0:
                        e.preload_act_table_set("natural_log_exp_and_others")
                    e.wait_ge(prj, g + 1)
                    if q % 8 >= 2:
                        e.wait_ge(qk_sum, q - 1)
                    else:
                        e.wait_ge(prj_free, NG // 2 * th + 20)
                    e.activation(prj_tmp[:, q % 2], bank[g % 3][:, :], ACT.Square).then_inc(qk_sq, 1)
                if g - 1 in QK:
                    q = QK.index(g - 1)
                    e.wait_ge(qk_sum, q + 1)
                    if q:
                        e.wait_ge(prj_free, QK[q - 1] + 1)
                    if q == 0:
                        e.wait_ge(eps_ok, 1)
                    e.activation(prj_std, bank[3][:, :], ACT.Ln, scale=1.0 / HD, bias=eps).then_inc(qk_ln, 1)
                    e.wait_ge(qk_ln, q + 1)
                    e.activation(prj_std, prj_std, ACT.Exp, scale=-0.5).then_inc(qk_inv, 1)
                if g in SPLIT:
                    upper_slab(SPLIT[g])
                if g in NORM:
                    square(NORM[g])
                if g in RSTEP:
                    th, t = RSTEP[g]
                    c = chunk_at(th, t - 1)
                    if c is not None:
                        e.wait_ge(r_acc, c + 1)
                        e.activation(state, bank[7][:, :], ACT.Copy).then_inc(r_state, 1)
                        e.wait_ge(r_o, c + 1)
                        if c:
                            e.wait_ge(r_ms, c)
                        e.activation(o_sq, o_buf[:, c % 2], ACT.Square).then_inc(r_osq, 1)
                        e.wait_ge(r_ms, c + 1)
                        if c >= 2:
                            e.wait_ge(r_norm, c - 1)
                        e.activation(ret_ss[:, 2 + c % 2, :], ret_ss[:, c % 2, :], ACT.Ln, scale=1.0 / P,
                                     bias=eps).then_inc(r_ln, 1)
                        e.wait_ge(r_ln, c + 1)
                        e.activation(ret_ss[:, 2 + c % 2, :], ret_ss[:, 2 + c % 2, :], ACT.Exp, scale=-0.5)\
                            .then_inc(r_inv, 1)
                    c = chunk_at(th, t)
                    if c is not None:
                        e.wait_ge(r_ktr, c + 1)
                        if c >= 2:
                            e.wait_ge(r_acc, c - 1)
                        e.activation(k_tok[:, c % 2], bank[4][:, :], ACT.Copy).then_inc(r_k, 1)

            def soft_plus(n):
                u = units[n]
                rng = slice(u["o0"], CH)
                e.wait_ge(z_ok, n + 1)
                if n >= 3:
                    e.wait_ge(z_sp, n - 2)
                e.activation(soft[:, n % 3, rng], bank[n % 4][:, rng], ACT.Abs).then_inc(z_abs, 1)
                e.wait_ge(z_abs, n + 1)
                e.activation(soft[:, n % 3, rng], soft[:, n % 3, rng], ACT.Exp, scale=-1.0).then_inc(z_exp, 1)
                e.wait_ge(z_exp, n + 1)
                e.activation(soft[:, n % 3, rng], soft[:, n % 3, rng], ACT.Ln, bias=1.0).then_inc(z_ln, 1)

            def weights(n):
                u = units[n]
                rng = slice(u["o0"], CH)
                e.wait_ge(z_cum, n + 1)
                if n >= 3:
                    e.wait_ge(z_pv, n - 2)
                e.activation(wgt[:, n % 3, rng], bank[n % 4][:, rng], ACT.Exp).then_inc(z_w, 1)

            e.wait_ge(r_mix, NT)
            e.preload_act_table_set("natural_log_exp_and_others")
            for n in range(NU + 2):
                if n < NU:
                    soft_plus(n)
                if n >= 2:
                    weights(n - 2)
            e.wait_ge(z_pv, NU)
            e.wait_ge(z_lo, NU)
            e.wait_ge(z_later, NU)
            for i in range(2):
                e.dma_start(x_re[:, i], xr[i]).then_inc(xr_in[i], 16)
            e.wait_ge(wo_in, 16)
            e.wait_ge(z_out, 16)
            for raw, upper, _lower in split_parts():
                e.activation(upper, raw, ACT.Copy).then_inc(es_hi, 1)
            for i in range(NT):
                e.wait_ge(e_x2, 2 * i + 2)
                if i + 2 < NT:
                    e.dma_start(x_re[:, i % 2], xr[i + 2]).then_inc(xr_in[i % 2], 16)
                if i:
                    e.wait_ge(e_sq, i)
                e.activation(e_dump, x2[:, i % 2], ACT.Square, accum_out=ssq2[:, i:i + 1]).then_inc(e_sq, 1)
                e.wait_ge(e_ms, i + 1)
                e.activation(ms2[:, i:i + 1], ms2[:, i:i + 1], ACT.Sqrt).then_inc(e_root, 1)
                e.wait_ge(e_inv, i + 1)
                if i >= 2:
                    e.wait_ge(e_tr, 2 * (i - 1))
                    e.wait_ge(e_st[i % 2], 32 * (i // 2))
                e.activation(xn2[:, i % 2], x2[:, i % 2], ACT.Copy, scale=rstd2[:, i:i + 1]).then_inc(e_norm, 1)
            e.wait_ge(f_step, 1)
            e.activation(f_w, f_w, ACT.Exp).then_inc(f_exp, 1)
            e.wait_ge(e_log, NT)
            e.wait_ge(e_st[0], 128)
            e.wait_ge(e_st[1], 128)
            e.dma_start(b_rows[:, 0:2048], b_gate_up[0]).then_inc(bias_in, 16)

            def weigh_rows(n):
                e.wait_ge(sc_done, n * 32 + 16)
                for h in range(2):
                    for q in range(2):
                        m = 2 * h + q
                        e.wait_ge(m_ytr, n * 4 + (m + 1))
                        e.activation(yo[:, h, q * 512:(q + 1) * 512], bank[4 + m][0:HC, :], ACT.Copy,
                                     scale=w_sc[:, h:h + 1]).then_inc(m_yo, 1)

            def block_act(n):
                for f in range(KD):
                    e.wait_ge(m_gate, n * 8 + (f + 1))
                    e.wait_ge(m_gs, n * 8 + (f + 1))
                    e.activation(sg[:, f % 2], g1[:, f % 2], ACT.Sigmoid, scale=GALPHA).then_inc(m_sig, 1)
                    if f == 0:
                        weigh_rows(n)

            with e.Fori(0, NE) as n:
                block_act(n)
            more = e.value_load(it_i[0:1, 1, NI - 1:NI], min_val=0, max_val=NX - 1)
            with e.If(more > 0):
                with e.Fori(NE, more + NE) as n:
                    block_act(n)
            weigh_rows(more + NE)

        @block.tensor
        def _(e):
            def turn_tile(i):
                e.wait_ge(a_norm, i + 1)
                for hf in range(2):
                    m = 2 * i + hf
                    if m >= 4:
                        e.wait_ge(a_hx, m - 3)
                    for q in range(4):
                        mm = e.transpose(bank[4 + m % 4][:, q * P:(q + 1) * P],
                                         x_norm[i % 2][:, (4 * hf + q) * P:(4 * hf + q + 1) * P], ident)
                    mm.then_inc(a_tr, 1)

            e.wait_ge(const_in, 16)
            turn_tile(0)
            e.wait_ge(vec_in, 16 * 7)
            e.transpose(bank[3][:, 0:V_N], vec_rows, cst[0:V_N, C_ID:C_ID + V_N]).then_inc(vec_tr, 1)
            def project(g):
                u = groups[g]
                b = u["slab"] % 2
                e.wait_ge(ws_lo, u["slab"] + 1)
                if g >= 3:
                    e.wait_ge(prj_free, g - 2)
                for k in range(KD):
                    if g in (0, NG // 2) and k % 2 == 0:
                        e.wait_ge(xs_lo, 4 * u["th"] + k // 2 + 1)
                    for xs, ws in ((x_hi, w_hi), (x_lo, w_hi), (x_hi, w_lo)):
                        if u["c"] in T_CHUNKS:
                            dst, lhs, rhs = bank[g % 3][:, :], ws[b][:, k, u["s"] * P:(u["s"] + 1) * P], xs[:, k, :]
                        else:
                            dst, lhs, rhs = bank[g % 3][:, 0:SL], xs[:, k, u["s"] * P:(u["s"] + 1) * P], ws[b][:, k, :]
                        mm = e.matmul(dst, lhs, rhs, start=k == 0 and (xs is x_hi and ws is w_hi),
                                      stop=k == KD - 1 and ws is w_lo)
                mm.then_inc(prj, 1)

            def head_sums(q):
                e.wait_ge(qk_sq, q + 1)
                if q:
                    e.wait_ge(qk_ln, q)
                e.matmul(bank[3][:, :], block_ones, prj_tmp[:, q % 2], start=True, stop=True).then_inc(qk_sum, 1)

            def retention(th, t):
                c = chunk_at(th, t - 2)
                if c is not None:
                    e.wait_ge(r_norm, c + 1)
                    e.wait_ge(r_k, HT * th + min(t, HT))
                    for h in range(RH):
                        mm = e.transpose(bank[4][:, h * P:(h + 1) * P], o_buf[:, c % 2, h * P:(h + 1) * P], ident)
                    mm.then_inc(r_tr, 1)
                c = chunk_at(th, t - 1)
                if c is not None:
                    i = c % HT
                    e.wait_ge(r_mask, c + 1)
                    e.wait_ge(r_k, c + 1)
                    if c:
                        e.wait_ge(r_o, c)
                        e.wait_ge(r_state, c)
                    for h in range(RH):
                        o = bank[6][:, h * P:(h + 1) * P]
                        mm = e.matmul(o, s_msk[:, c % 2, h * P:(h + 1) * P], rv[:, i, h * P:(h + 1) * P],
                                      start=True, stop=c == 0)
                        if c:
                            mm = e.matmul(o, rqT[:, h, i * P:(i + 1) * P], state[:, h * P:(h + 1) * P],
                                          start=False, stop=True)
                    mm.then_inc(r_out, 1)
                    for h in range(RH):
                        mm = e.matmul(bank[7][:, h * P:(h + 1) * P], k_tok[:, c % 2, h * P:(h + 1) * P],
                                      rv[:, i, h * P:(h + 1) * P], start=c == 0 and h == 0, stop=True,
                                      skip_group_check=True)
                    mm.then_inc(r_acc, 1)
                c = chunk_at(th, t)
                if c is not None:
                    if t == 0:
                        e.wait_ge(rope_ok, 2 * RH * (th + 1))
                        e.wait_ge(prj_free, NG // 2 * th + 16)
                    if c:
                        e.wait_ge(r_mask, c)
                    for h in range(RH):
                        mm = e.matmul(bank[5][:, h * P:(h + 1) * P], rkT[:, h, t * P:(t + 1) * P],
                                      rqT[:, h, t * P:(t + 1) * P], start=True, stop=True)
                    mm.then_inc(r_score, 1)
                    back = HT * th + max(0, t - 1)
                    if back:
                        e.wait_ge(r_mix, back)
                    if c:
                        e.wait_ge(r_k, c)
                    if th == 0 and t == 0:
                        e.wait_ge(a_hx, 2 * NT)
                    for h in range(RH):
                        mm = e.transpose(bank[4][:, h * P:(h + 1) * P], rkT[:, h, t * P:(t + 1) * P], ident)
                    mm.then_inc(r_ktr, 1)

            for i in range(1, HT):
                turn_tile(i)
            for g in range(NG):
                project(g)
                if g - 1 in QK:
                    head_sums(QK.index(g - 1))
                if g in TURN:
                    turn_tile(TURN[g])
                if g in RSTEP:
                    retention(*RSTEP[g])

            def score_unit(n):
                u = units[n]
                pr = slice(HD * (u["h"] % 2), HD * (u["h"] % 2) + HD)
                if n >= 4:
                    e.wait_ge(z_w, n - 3)
                b, par = u["h"] // 2 % 2, u["par"]
                e.wait_ge(z_st, 10 * (u["h"] // 2 + 1))
                keys, queries = slice(u["b"] * P, (u["b"] + 1) * P), slice(u["t0"], (u["th"] + 1) * CH)
                e.matmul(bank[n % 4][:, u["o0"]:CH], k_st[b][:, par, keys], q_st[b][:, par, queries],
                         start=True, stop=False, skip_group_check=True)
                mm = e.matmul(bank[n % 4][:, u["o0"]:CH], k_st[b][pr, par, keys], q_low[b][pr, queries],
                              start=False, stop=False, skip_group_check=True)
                if u["diag"]:
                    mm = e.matmul(bank[n % 4][:, u["o0"]:u["o0"] + P], ident_r, mask_r, start=False,
                                  stop=False, skip_group_check=True)
                mm.then_inc(z_ok, 1)

            def cumulate(n):
                u = units[n]
                cols = slice(u["o0"], CH)
                if not u["first"]:
                    e.wait_ge(z_sp, n + 1)
                    e.wait_ge(z_later, n - 1)
                    e.matmul(bank[n % 4][:, cols], neg_ones, later[:, u["par"], u["step"] % 2, cols],
                             start=False, stop=False, skip_group_check=True)
                e.wait_ge(z_hi, n + 1)
                e.matmul(bank[n % 4][:, cols], neg_upper_r, sp_hi[:, n % 3, cols], start=False,
                         stop=False, skip_group_check=True)
                e.wait_ge(z_lo, n + 1)
                e.matmul(bank[n % 4][:, cols], neg_upper_r, sp_lo[:, n % 3, cols], start=False,
                         stop=True, skip_group_check=True).then_inc(z_cum, 1)

            def values(n):
                u = units[n]
                pr = slice(HD * (u["h"] % 2), HD * (u["h"] % 2) + HD)
                e.wait_ge(z_w, n + 1)
                if u["first"] and u["chain"] >= 2:
                    e.wait_ge(z_out, nth(of_chain(u["par"], u["chain"] - 2, "last"), "last"))
                e.matmul(out_bank(u)[pr, u["o0"]:CH], sv[:, u["b"], u["h"] * HD:(u["h"] + 1) * HD],
                         wgt[:, n % 3, u["o0"]:CH], start=u["first"], stop=u["last"],
                         skip_group_check=True).then_inc(z_pv, 1)

            e.wait_ge(prj_free, NG)
            e.wait_ge(r_mix, NT)
            e.wait_ge(r_state, NT)
            e.wait_ge(z_const, 3)
            for n in range(-2, NU + 2):
                if 0 <= n + 2 < NU:
                    score_unit(n + 2)
                if n >= 2:
                    values(n - 2)
                if 0 <= n < NU:
                    cumulate(n)

            e.wait_ge(wo_in, 16)
            e.wait_ge(z_out, 16)
            e.wait_ge(rt_in, 32)

            def out_proj(i):
                for nh in range(2):
                    g = 2 * i + nh
                    if g >= 4:
                        e.wait_ge(e_x2, g - 3)
                    for k in range(KD):
                        if i == 0:
                            e.wait_ge(es_lo, 10 + k + 1 if nh else (2 if k == 0 else k + 3))
                        elif nh == 0 and k == 0:
                            e.wait_ge(es_lo, 18 + 2 * i)
                        tokens, cols = slice(i * P, (i + 1) * P), slice(nh * CH, (nh + 1) * CH)
                        e.matmul(bank[g % 4][:, :], mix_hi[:, k, tokens], wo_hi[:, k, cols], start=k == 0, stop=False)
                        e.matmul(bank[g % 4][:, :], mix_lo[:, k, tokens], wo_hi[:, k, cols], start=False, stop=False)
                        mm = e.matmul(bank[g % 4][:, :], mix_hi[:, k, tokens], wo_lo[:, k, cols], start=False,
                                      stop=k == KD - 1)
                    mm.then_inc(e_prj, 1)

            def turn(i):
                e.wait_ge(e_norm, i + 1)
                for hf in range(2):
                    if i:
                        e.wait_ge(e_xf, 2 * i - 1 + hf)
                    for q in range(4):
                        k = 4 * hf + q
                        mm = e.transpose(bank[4 + hf][:, q * P:(q + 1) * P], xn2[:, i % 2, k * P:(k + 1) * P], ident)
                    mm.then_inc(e_tr, 1)

            def route(i):
                e.wait_ge(e_xf, 2 * i + 2)
                if i:
                    e.wait_ge(e_logb, 6 * i - 5)
                for k in range(KD):
                    mm = e.matmul(bank[6][:, 0:NE], xfT[:, i % 2, k, :], wr[:, k, :], start=k == 0, stop=k == KD - 1)
                mm.then_inc(e_log, 1)

            for i in range(NT + 2):
                if i < NT:
                    out_proj(i)
                if 1 <= i <= NT:
                    turn(i - 1)
                if 2 <= i:
                    route(i - 2)
            e.wait_ge(b_ok, 2)
            e.wait_ge(e_logb, 6 * NT)
            e.matmul(bank[2][:, 0:NT * NE], before_b, f_m.rearrange("p i e -> p (i e)"), start=True, stop=False,
                     skip_group_check=True)
            for j in range(NT - 1):
                n = NT - 1 - j
                mm = e.matmul(bank[2][:, (j + 1) * NE:NT * NE].rearrange("p (i e) -> p i e", e=NE), ones_b,
                              f_m[:, j:j + 1, :].to_broadcast([P, n, NE]), start=False, stop=j == NT - 2,
                              skip_group_check=True)
            for j in range(NT):
                mm = e.matmul(bank[3][:, 0:NE], ones_b, f_m[:, j, :], start=j == 0, stop=j == NT - 1)
            mm.then_inc(f_rank, 1)

            def token_list():
                for h in range(2):
                    for i in range(NT):
                        mm = e.matmul(bank[7][0:HC, 5 * h:5 * h + 5], hot[:, i, h * HC:(h + 1) * HC], tw_s[:, i, :],
                                      start=i == 0, stop=i == NT - 1)
                mm.then_inc(l_sum, 1)

            def turn_tokens():
                for k in range(KD):
                    for h in range(2):
                        at = (k % 3) * CAP + h * HC
                        mm = e.transpose(bank[4 + k // 3][:, at:at + HC], xg[:, h, k * P:(k + 1) * P],
                                         cst[0:HC, C_ID:C_ID + HC])
                    if k in (2, 5, 7):
                        mm.then_inc(g_tr, 1)

            e.wait_ge(l_hot, 1)
            token_list()
            e.wait_ge(bias_in, 16)
            e.wait_ge(sc_done, 16)
            e.wait_ge(e_x2, 16)
            for j in range(24):
                if j < 16:
                    src = b_rows[:, (j % 8) * 256 + j // 8:(j % 8) * 256 + 256:2]
                else:
                    src = b_rows[:, 2048 + (j - 16) * P:2048 + (j - 15) * P]
                mm = e.transpose(bank[j // 12][:, (j % 12) * NE:(j % 12 + 1) * NE], src, cst[0:NE, C_ID:C_ID + NE])
            mm.then_inc(bias_tr, 1)
            e.wait_ge(bias_ok, 3)
            e.wait_ge(g_in, 32)
            turn_tokens()

            def turn_rows(n):
                e.wait_ge(m_y, n * 8 + 2)
                e.wait_ge(l_ok, n + 1)
                for h in range(2):
                    for q in range(2):
                        for r in range(4):
                            mm = e.transpose(bank[4 + 2 * h + q][0:HC, r * P:(r + 1) * P],
                                             yT[:, 4 * q + r, h * HC:(h + 1) * HC], ident)
                        mm.then_inc(m_ytr, 1)

            def block_matmuls(n, w):
                e.wait_ge(g_xT, n * 3 + 3)
                for f in range(KD):
                    if f % 2 == 0:
                        e.wait_ge(gu_in[f // 2], n * 16 + 16)
                    e.wait_ge(m_up, n * 8 + (f + 1))
                    for part in range(2):
                        for k in range(KD):
                            mm = e.matmul(bank[f % 2][:, part * CAP:part * CAP + w],
                                          gu_ring[:, k, f * 256 + part:(f + 1) * 256:2], xT[:, k, 0:w],
                                          start=k == 0, stop=k == KD - 1)
                    mm.then_inc(m_gu, 1)
                    if f == 0:
                        turn_rows(n)
                    if f == 5:
                        e.wait_ge(l_hot, n + 2)
                        e.wait_ge(m_yo, n * 4 + 4)
                        token_list()
                def down(j, k):
                    return e.matmul(bank[2 + j % 2][:, 0:w], dn_ring[:, k, j * P:(j + 1) * P], hid[:, k, 0:w],
                                    start=k == 0, stop=k == KD - 1)

                e.wait_ge(dn_in[0], n * 16 + 16)
                e.wait_ge(m_hid, n * 8 + 9)
                e.wait_ge(m_y, n * 8 + 1)
                for k in range(KD - 1):
                    down(0, k)
                e.wait_ge(m_y, n * 8 + 2)
                for k in range(KD // 2):
                    down(1, k)
                e.wait_ge(m_hid, n * 8 + 10)
                down(0, KD - 1).then_inc(m_dn, 1)
                for k in range(KD // 2, KD):
                    mm = down(1, k)
                mm.then_inc(m_dn, 1)
                for j in range(2, KD):
                    if j == 4:
                        e.wait_ge(dn_in[1], n * 16 + 16)
                    e.wait_ge(m_y, n * 8 + (j + 1))
                    for k in range(KD):
                        mm = down(j, k)
                    mm.then_inc(m_dn, 1)
                    if j == 5:
                        e.wait_ge(g_in, n * 32 + 64)
                        e.wait_ge(m_yo, n * 4 + 4)
                        turn_tokens()

            def block_pe(n):
                tokens = e.value_load(it_i[0:1, 1, bass.ds(n, 1)], min_val=-S, max_val=S)

                def choose(widths):
                    if len(widths) == 1:
                        block_matmuls(n, widths[0])
                        return
                    half = len(widths) // 2
                    with e.If(tokens <= widths[half - 1]):
                        choose(widths[:half])
                    with e.Else():
                        choose(widths[half:])

                choose(WIDTHS)

            e.wait_ge(it_step, 1)
            with e.Fori(0, NE) as n:
                block_pe(n)
            more = e.value_load(it_i[0:1, 1, NI - 1:NI], min_val=0, max_val=NX - 1)
            with e.If(more > 0):
                with e.Fori(NE, more + NE) as n:
                    block_pe(n)
            turn_rows(more + NE)

        @block.vector
        def _(e):

            def normalise(i):
                e.wait_ge(a_sq, i + 1)
                e.tensor_scalar(ms[:, i:i + 1], ssq[:, i:i + 1], 1.0 / D, EPS, ALU.mult, ALU.add).then_inc(a_ms, 1)
                e.wait_ge(a_root, i + 1)
                e.reciprocal(rstd[:, i:i + 1], ms[:, i:i + 1]).then_inc(a_inv, 1)
                e.wait_ge(a_inv, i + 1)
                if i >= 2:
                    e.wait_ge(a_tr, 2 * i - 2)
                e.tensor_scalar(x_norm[i % 2], x_in[i % HT], rstd[:, i:i + 1], None, ALU.mult).then_inc(a_norm, 1)

            def to_raw(i):
                if i >= HT:
                    e.wait_ge(xs_lo, KD // 2)
                for hf in range(2):
                    e.wait_ge(a_tr, 2 * i + hf + 1)
                    g = vecs[:, V_AG + 4 * hf:V_AG + 4 * hf + 4]
                    e.tensor_tensor(x_raw[:, 4 * hf:4 * hf + 4, (i % HT) * P:(i % HT + 1) * P],
                                    bank[4 + (2 * i + hf) % 4][:, :].rearrange("p (k t) -> p k t", t=P),
                                    g.unsqueeze(2).to_broadcast([P, 4, P]), ALU.mult).then_inc(a_hx, 1)

            def lower_slab(j):
                e.wait_ge(ws_hi, j + 1)
                e.tensor_tensor(w_lo[j % 2], w_raw[j % 2], w_hi[j % 2].bitcast(F32), ALU.subtract).then_inc(ws_lo, 1)

            def lower_tokens(th):
                for q in range(KD // 2):
                    e.wait_ge(xs_hi, KD // 2 * th + q + 1)
                    e.tensor_tensor(x_lo[:, 2 * q:2 * q + 2], x_raw[:, 2 * q:2 * q + 2],
                                    x_hi[:, 2 * q:2 * q + 2].bitcast(F32), ALU.subtract).then_inc(xs_lo, 1)

            normalise(0)
            e.memset(eps, EPS).then_inc(eps_ok, 1)
            e.wait_ge(vec_tr, 1)
            e.tensor_copy(vecs, bank[3][:, 0:V_N]).then_inc(vec_ok, 1)
            e.wait_ge(vec_ok, 1)
            e.tensor_scalar(sbq_g, vecs[:, V_SQ:V_SQ + 1], HD ** -0.5, None, ALU.mult).then_inc(vec_ok, 1)
            for i in range(1, HT):
                normalise(i)
                to_raw(i - 1)
            lower_slab(0)
            to_raw(HT - 1)
            lower_tokens(0)

            def qk_norm(q):
                u = groups[QK[q]]
                c, th = u["c"], u["th"]
                dst = (sqT if c == 4 else skT)[:, u["row"], th * CH:(th + 1) * CH]
                gv = sbq_g if c == 4 else vecs[:, V_SK:V_SK + 1]
                e.wait_ge(qk_inv, q + 1)
                e.scalar_tensor_tensor(dst, bank[QK[q] % 3][:, :], gv, prj_std, ALU.mult, ALU.mult).then_inc(prj_free, 1)

            def retention(th, t):
                c = chunk_at(th, t - 1)
                if c is not None:
                    e.wait_ge(r_out, c + 1)
                    if c >= 2:
                        e.wait_ge(r_tr, c - 1)
                    e.tensor_tensor(o_buf[:, c % 2].rearrange("p (h n) -> p h n", h=RH),
                                    bank[6][:, :].rearrange("p (h n) -> p h n", h=RH),
                                    g_o[:, c, :].unsqueeze(2).to_broadcast([P, RH, P]), ALU.mult).then_inc(r_o, 1)
                c = chunk_at(th, t)
                if c is not None:
                    e.wait_ge(r_score, c + 1)
                    if c >= 2:
                        e.wait_ge(r_out, c - 1)
                    e.tensor_tensor(s_msk[:, c % 2].rearrange("p (h n) -> p h n", h=RH),
                                    bank[5][:, :].rearrange("p (h n) -> p h n", h=RH),
                                    causal.unsqueeze(1).to_broadcast([P, RH, P]), ALU.mult).then_inc(r_mask, 1)
                c = chunk_at(th, t - 2)
                if c is not None:
                    e.wait_ge(r_tr, c + 1)
                    dst = mixT[:, 0:RH, c * P:(c + 1) * P]
                    e.tensor_tensor(dst, bank[4][:, :].rearrange("p (h n) -> p h n", h=RH), dst,
                                    ALU.mult).then_inc(r_mix, 1)
                c = chunk_at(th, t - 1)
                if c is not None:
                    e.wait_ge(r_osq, c + 1)
                    if c >= 2:
                        e.wait_ge(r_ln, c - 1)
                    e.tensor_reduce(ret_ss[:, c % 2, :], o_sq.rearrange("p (h n) -> p h n", h=RH), X, ALU.add).then_inc(r_ms, 1)

            def pair_step(p, j):
                b = p % 2
                q, k, low = sqT[:, p, :], skT[:, p, :], q_low[b]
                ks, qs = k_st[b], q_st[b]
                one, two = slice(0, HD), slice(HD, P)
                dst, src, upper = (
                    (ks[one, 0], k[one], None), (ks[two, 1], k[two], None),
                    (qs[one, 0], q[one], None), (qs[two, 1], q[two], None),
                    (qs[two, 0], q[one], None), (qs[one, 1], q[two], None),
                    (ks[two, 0], k[one], ks[one, 0]), (ks[one, 1], k[two], ks[two, 1]),
                    (low[one], q[one], qs[one, 0]), (low[two], q[two], qs[two, 1]))[j]
                if upper is None:
                    e.tensor_copy(dst, src).then_inc(z_st, 1)
                else:
                    e.wait_ge(z_st, 10 * p + 4)
                    e.tensor_tensor(dst, src, upper.bitcast(F32), ALU.subtract).then_inc(z_st, 1)

            for g, u in enumerate(groups):
                th, c, s = u["th"], u["c"], u["s"]
                src = bank[g % 3][:, :]
                if g == NG // 2:
                    lower_tokens(1)
                    e.wait_ge(rope_in, 32)
                    e.wait_ge(r_acc, HT)
                    e.wait_ge(qk_sum, 8)
                if c in (0, 1):
                    q = RH * c + u["row"]
                    dst = (rqT if c == 0 else rkT)[:, u["row"], :]
                    t = prj_tmp[:, q % 2]
                    e.wait_ge(prj, g + 1)
                    if g == 0:
                        e.wait_ge(rope_in, 16)
                        e.wait_ge(const_in, 16)
                    if q >= 2:
                        e.wait_ge(rope_ok, 2 * RH * th + q - 1)
                    e.tensor_tensor(t[0:64], src[64:128], rope_t[64:128, 1, :], ALU.mult)
                    e.tensor_tensor(t[64:128], src[0:64], rope_t[0:64, 1, :], ALU.mult)
                    e.tensor_tensor(dst, src, rope_t[:, 0, :], ALU.mult).then_inc(prj_free, 1)
                elif c == 2:
                    h0 = 2 * (u["slab"] % 2)
                    e.wait_ge(prj, g + 1)
                    e.tensor_tensor(rv[:, s, h0 * P:(h0 + 2) * P].rearrange("p (h n) -> p h n", h=2),
                                    src[:, 0:SL].rearrange("p (h n) -> p h n", h=2),
                                    g_v[:, HT * th + s, h0:h0 + 2].unsqueeze(2).to_broadcast([P, 2, P]),
                                    ALU.mult).then_inc(prj_free, 1)
                elif c == 3:
                    e.wait_ge(gate_sig, RH * th + u["row"] + 1)
                    e.scalar_tensor_tensor(mixT[:, u["row"], th * CH:(th + 1) * CH], src,
                                           vecs[:, V_RG + u["row"]:V_RG + u["row"] + 1], prj_tmp[:, g % 2],
                                           ALU.mult, ALU.mult).then_inc(prj_free, 1)
                if g - 1 in QK:
                    qk_norm(QK.index(g - 1))
                if c == 6:
                    e.wait_ge(prj, g + 1)
                    at = SL * (u["slab"] % 2)
                    e.tensor_copy(sv[:, HT * th + s, at:at + SL], src[:, 0:SL]).then_inc(prj_free, 1)
                if g in SPLIT:
                    lower_slab(SPLIT[g])
                if NG - 7 <= g < NG - 2:
                    if g == NG - 7:
                        e.wait_ge(prj_free, NG - 8)
                    for j in range(2):
                        pair_step(0, 2 * (g - NG + 7) + j)
                if g in TURN:
                    to_raw(TURN[g])
                if g in NORM:
                    normalise(NORM[g])
                if g in RSTEP:
                    retention(*RSTEP[g])

            def softplus(n):
                u = units[n]
                rng = slice(u["o0"], CH)
                e.wait_ge(z_ln, n + 1)
                if n >= 3:
                    e.wait_ge(z_lo, n - 2)
                    e.wait_ge(z_later, n - 2)
                e.scalar_tensor_tensor(sp[:, n % 3, rng], bank[n % 4][:, rng], 0.0, soft[:, n % 3, rng],
                                       ALU.max, ALU.add).then_inc(z_sp, 1)

            def chain_out(n):
                u = units[n]
                pr = slice(HD * (u["h"] % 2), HD * (u["h"] % 2) + HD)
                e.wait_ge(z_pv, n + 1)
                e.tensor_copy(mixT[pr, RH + u["h"] // 2, u["th"] * CH:(u["th"] + 1) * CH],
                              out_bank(u)[pr, :]).then_inc(z_out, 1)

            def parts(n):
                rng = slice(units[n]["o0"], CH)
                e.wait_ge(z_sp, n + 1)
                if n >= 3:
                    e.wait_ge(z_cum, n - 2)
                e.tensor_copy(sp_hi[:, n % 3, rng], sp[:, n % 3, rng]).then_inc(z_hi, 1)
                e.wait_ge(z_hi, n + 1)
                e.tensor_tensor(sp_lo[:, n % 3, rng], sp[:, n % 3, rng], sp_hi[:, n % 3, rng].bitcast(F32),
                                ALU.subtract).then_inc(z_lo, 1)

            e.tensor_copy(neg_upper_r, neg_upper).then_inc(z_const, 1)
            e.tensor_copy(ident_r, ident).then_inc(z_const, 1)
            e.tensor_copy(mask_r, mask_bias).then_inc(z_const, 1)
            for n in range(NU + 4):
                if n < NU:
                    softplus(n)
                    parts(n)
                    p, j = n // PAIR + 1, n % PAIR - 3
                    if p < SH // 2 and 0 <= j < 20 and j % 2 == 0:
                        if j == 0 and p >= 2:
                            e.wait_ge(z_ok, PAIR * (p - 1))
                        pair_step(p, j // 2)
                if n >= 4 and units[n - 4]["last"]:
                    chain_out(n - 4)

            e.wait_ge(z_later, NU)

            def residual(i):
                e.wait_ge(xr_in[i % 2], 16 * (i // 2 + 1))
                if i >= 2:
                    e.wait_ge(e_norm, i - 1)
                    e.wait_ge(e_st[i % 2], 32 * (i // 2))
                for nh in range(2):
                    g = 2 * i + nh
                    e.wait_ge(e_prj, g + 1)
                    e.tensor_tensor(x2[:, i % 2, nh * CH:(nh + 1) * CH], bank[g % 4][:, :],
                                    x_re[:, i % 2, nh * CH:(nh + 1) * CH], ALU.add).then_inc(e_x2, 1)
                e.wait_ge(e_sq, i + 1)
                e.tensor_scalar(ms2[:, i:i + 1], ssq2[:, i:i + 1], 1.0 / D, EPS, ALU.mult, ALU.add).then_inc(e_ms, 1)
                e.wait_ge(e_root, i + 1)
                e.reciprocal(rstd2[:, i:i + 1], ms2[:, i:i + 1]).then_inc(e_inv, 1)

            def scaled(i):
                for hf in range(2):
                    e.wait_ge(e_tr, 2 * i + hf + 1)
                    if i >= 2:
                        e.wait_ge(e_log, i - 1)
                    g = vecs[:, V_FG + 4 * hf:V_FG + 4 * hf + 4]
                    e.tensor_tensor(xfT[:, i % 2, 4 * hf:4 * hf + 4, :],
                                    bank[4 + hf][:, :].rearrange("p (k t) -> p k t", t=P),
                                    g.unsqueeze(2).to_broadcast([P, 4, P]), ALU.mult).then_inc(e_xf, 1)

            def best(i):
                e.wait_ge(e_log, i + 1)
                e.tensor_tensor(logits[:, i, :], bank[6][:, 0:NE], brt, ALU.add).then_inc(e_logb, 1)
                e.wait_ge(e_logb, 6 * i + 1)
                e.max(top_v[:, i, :], logits[:, i, :]).then_inc(e_logb, 1)
                e.wait_ge(e_logb, 6 * i + 2)
                e.max_index(top_i[:, i, :].bitcast(U32), top_v[:, i, :], logits[:, i, :]).then_inc(e_logb, 1)
                e.wait_ge(e_logb, 6 * i + 3)
                e.tensor_copy(f_i, top_i[:, i, :].bitcast(U32)).then_inc(e_logb, 1)
                e.wait_ge(e_logb, 6 * i + 4)
                e.tensor_tensor(f_a[:, i], f_i[:, 0:4].unsqueeze(2).to_broadcast([P, 4, NE]),
                                iota_e.unsqueeze(1).to_broadcast([P, 4, NE]), ALU.is_equal).then_inc(e_logb, 1)
                e.wait_ge(e_logb, 6 * i + 5)
                e.tensor_reduce(f_m[:, i, :], f_a[:, i].rearrange("p k e -> p e k"), X, ALU.add).then_inc(e_logb, 1)

            e.tensor_copy(before_b, before).then_inc(b_ok, 1)
            e.tensor_copy(ones_b, ones).then_inc(b_ok, 1)
            e.wait_ge(rt_in, 32)
            done = [0]

            def split(upto):
                for raw, upper, lower in list(split_parts())[done[0]:upto]:
                    done[0] += 1
                    e.wait_ge(es_hi, done[0])
                    e.tensor_tensor(lower, raw, upper.bitcast(F32), ALU.subtract).then_inc(es_lo, 1)

            split(20)
            for i in range(NT + 2):
                split(min(22 + 2 * i, 18 + 2 * NT))
                if i < NT:
                    residual(i)
                if 1 <= i <= NT:
                    scaled(i - 1)
                if 2 <= i:
                    best(i - 2)

            count = [0]

            def step(ins):
                count[0] += 1
                ins.then_inc(f_step, 1)
                e.wait_ge(f_step, count[0])

            wide = [P, NT, 4, NE]
            e.wait_ge(e_logb, 6 * NT)
            step(e.tensor_tensor(f_w, top_v[:, :, 0:4], top_v[:, :, 0:1].to_broadcast([P, NT, 4]), ALU.subtract))
            e.wait_ge(f_exp, 1)
            step(e.tensor_reduce(f_s, f_w, X, ALU.add))
            step(e.reciprocal(f_s, f_s))
            step(e.tensor_tensor(f_w, f_w, f_s.unsqueeze(2).to_broadcast([P, NT, 4]), ALU.mult))
            step(e.tensor_tensor(f_b, f_a, f_w.unsqueeze(3).to_broadcast(wide), ALU.mult))
            three = [P, NT, NE]
            step(e.tensor_reduce(f_t, f_b.rearrange("p i k e -> p i e k"), X, ALU.add))
            step(e.tensor_copy(twx[:, :, 0:NE, 0], f_t))
            step(e.tensor_tensor(f_t, f_t, twx[:, :, 0:NE, 0], ALU.subtract))
            step(e.tensor_copy(twx[:, :, 0:NE, 1], f_t))
            step(e.tensor_tensor(f_t, f_t, twx[:, :, 0:NE, 1], ALU.subtract))
            step(e.tensor_copy(twx[:, :, 0:NE, 2], f_t))
            step(e.memset(twx[:, :, NE, :], 0.0))
            e.wait_ge(f_rank, 1)
            step(e.tensor_copy(f_r, bank[2][:, 0:NT * NE].rearrange("p (i e) -> p i e", e=NE)))
            step(e.tensor_tensor(f_c, bank[3][:, 0:NE].unsqueeze(1).to_broadcast(three),
                                 tok_id.unsqueeze(2).to_broadcast(three), ALU.add))
            step(e.scalar_tensor_tensor(f_c, f_r, -2.0, f_c, ALU.mult, ALU.add))
            step(e.tensor_scalar(f_n, f_m, -1.0, 1.0, ALU.mult, ALU.add))
            step(e.tensor_tensor(f_c, f_c, f_n, ALU.mult))
            step(e.tensor_tensor(pos[:, :, 0:NE], f_r, f_c, ALU.add))
            step(e.tensor_copy(pos[:, :, NE:NE + 1], tok_id.unsqueeze(2)))

            def list_hot(n, x_e):
                e.tensor_scalar(pos_s, pos[:, :, bass.ds(x_e, 1)].rearrange("p i o -> p (i o)"), it_base[:, bass.ds(n, 1)],
                                None, ALU.subtract).then_inc(l_pos, 1)
                e.scalar_tensor_tensor(tw_s[:, :, 2:5], pos[:, :, bass.ds(x_e, 1)].to_broadcast([P, NT, 3]),
                                       it_low[:, bass.ds(n, 1)],
                                       twx[:, :, bass.ds(x_e, 1), :].rearrange("p i o c -> p i (o c)"), ALU.is_ge, ALU.mult)
                e.wait_ge(l_pos, n + 1)
                e.tensor_tensor(hot, pos_s.unsqueeze(2).to_broadcast([P, NT, CAP]),
                                iota_cap.unsqueeze(1).to_broadcast([P, NT, CAP]), ALU.is_equal).then_inc(l_hot, 1)

            def list_out(n):
                sums = bank[7][0:HC, 0:10].rearrange("p (h c) -> p h c", c=5)
                e.tensor_reduce(l_raw, sums[:, :, 0:2], X, ALU.add).then_inc(l_id, 1)
                e.tensor_reduce(wsel, sums[:, :, 2:5], X, ALU.add)
                e.wait_ge(l_id, n + 1)
                e.tensor_copy(idx, l_raw).then_inc(l_ok, 1)

            def tokens_out(m):
                n = 3 if m < 2 else 2
                g = vecs[:, V_FG + 3 * m:V_FG + 3 * m + n]
                e.tensor_tensor(xT[:, 3 * m:3 * m + n, :], bank[4 + m][:, 0:n * CAP].rearrange("p (k t) -> p k t", t=CAP),
                                g.unsqueeze(2).to_broadcast([P, n, CAP]), ALU.mult).then_inc(g_xT, 1)

            built = [0]

            def table(ins):
                built[0] += 1
                ins.then_inc(it_step, 1)
                e.wait_ge(it_step, built[0])

            e.tensor_copy(f_cnt, bank[3][:, 0:NE])
            e.tensor_copy(tw_s[:, :, 0], tile_at)
            e.tensor_copy(tw_s[:, :, 1], tok_id[:, 0:1].to_broadcast([P, NT]))
            e.memset(it_base, 0.0)
            e.memset(it_low, 0.0)
            table(e.tensor_copy(it_i[:, 1, 0:NE], bank[3][:, 0:NE]))
            list_hot(0, 0)
            e.wait_ge(l_sum, 1)
            list_out(0)
            e.wait_ge(l_ok, 1)
            e.tensor_copy(idx_sc, idx)
            e.memset(w_sc, 0.0)
            e.memset(yT, 0.0).then_inc(m_y, 2)
            e.wait_ge(bias_tr, 1)
            for m in range(2):
                e.tensor_copy(btab[:, :, 12 * m:12 * m + 12],
                              bank[m][:, 0:12 * NE].rearrange("p (j e) -> p e j", e=NE)).then_inc(bias_ok, 1)
            e.wait_ge(bias_ok, 2)
            e.tensor_scalar(btab[:, :, 8:16], btab[:, :, 8:16], 1.0, None, ALU.add).then_inc(bias_ok, 1)
            e.wait_ge(bias_ok, 3)
            for m in range(3):
                e.wait_ge(g_tr, m + 1)
                tokens_out(m)
            for s_ in (m_up, m_gs, m_hid):
                e.sem_inc(s_, 2)
            grid = [P, NX, NE]
            few = region(work, 0, NE, NB1)
            table(e.tensor_tensor(few, f_cnt.unsqueeze(2).to_broadcast([P, NE, NB1]),
                                  further.unsqueeze(1).to_broadcast([P, NE, NB1]), ALU.is_gt))
            table(e.tensor_reduce(f_over, few, X, ALU.add))
            table(e.tensor_tensor_scan(f_cum, ones[:, 0:NE], f_over, 0.0, ALU.mult, ALU.add))
            table(e.tensor_tensor(f_x, f_cum.unsqueeze(1).to_broadcast(grid), iota_x.unsqueeze(2).to_broadcast(grid),
                                  ALU.is_le))
            table(e.tensor_reduce(it_f[:, 0, NE:NI], f_x, X, ALU.add))
            table(e.tensor_tensor(f_y, f_x, f_over.unsqueeze(1).to_broadcast(grid), ALU.mult))
            table(e.tensor_reduce(f_prior, f_y, X, ALU.add))
            table(e.tensor_tensor(f_prior, iota_x, f_prior, ALU.subtract))
            table(e.tensor_scalar(it_low[:, NE:NI], f_prior, float(CAP), float(CAP), ALU.mult, ALU.add))
            table(e.tensor_scalar(it_base[:, NE:NI], it_low[:, NE:NI], float(S - CAP), None, ALU.min))
            table(e.tensor_tensor(f_x, it_f[:, 0, NE:NI].unsqueeze(2).to_broadcast(grid),
                                  iota_e.unsqueeze(1).to_broadcast(grid), ALU.is_equal))
            table(e.tensor_tensor(f_y, f_x, f_cnt.unsqueeze(1).to_broadcast(grid), ALU.mult))
            table(e.tensor_reduce(f_prior, f_y, X, ALU.add))
            table(e.tensor_tensor(it_f[:, 1, NE:NI], f_prior, it_base[:, NE:NI], ALU.subtract))
            table(e.tensor_copy(it_f[:, 1, NI - 1:NI], f_cum[:, NE - 1:NE]))
            table(e.tensor_copy(it_f[:, 0, 0:NE], iota_e))
            e.tensor_copy(it_i[:, 0, :], it_f[:, 0, :])
            table(e.tensor_copy(it_i[:, 1, NE:NI], it_f[:, 1, NE:NI]))
            assert built[0] == IT_STEPS

            def block_dve(n, x_e):
                e.wait_ge(m_y, n * 8 + 2)
                e.tensor_copy(be, btab[:, bass.ds(x_e, 1), :].rearrange("p o j -> p (o j)")).then_inc(m_bias, 1)
                e.wait_ge(m_bias, n + 1)
                for f in range(KD):
                    b = f % 2
                    e.wait_ge(m_gu, n * 8 + (f + 1))
                    e.wait_ge(m_hid, n * 8 + (f + 1))
                    e.tensor_scalar(g1[:, b], bank[b][:, 0:CAP], be[:, f:f + 1], GLIM, ALU.add, ALU.min)\
                        .then_inc(m_gate, 1)
                    e.tensor_scalar(u1[:, b], bank[b][:, CAP:2 * CAP], be[:, 8 + f:9 + f], GLIM + 1.0,
                                    ALU.add, ALU.min).then_inc(m_up, 1)
                    e.wait_ge(m_sig, n * 8 + (f + 1))
                    e.wait_ge(m_up, n * 8 + (f + 3))
                    e.tensor_tensor(gs[:, b], g1[:, b], sg[:, b], ALU.mult).then_inc(m_gs, 1)
                    e.wait_ge(m_gs, n * 8 + (f + 3))
                    e.scalar_tensor_tensor(hid[:, f, :], u1[:, b], 1.0 - GLIM, gs[:, b], ALU.max, ALU.mult)\
                        .then_inc(m_hid, 1)
                    if f == 2:
                        e.wait_ge(l_sum, n + 1)
                        list_hot(n + 1, e.value_load(it_i[0:1, 0, bass.ds(n + 1, 1)], min_val=0, max_val=NE))
                    if f == 6:
                        e.wait_ge(l_ok, n + 1)
                        e.wait_ge(m_yo, n * 4 + 4)
                        e.wait_ge(sc_done, n * 32 + 48)
                        e.tensor_copy(idx_sc, idx)
                        e.tensor_copy(w_sc, wsel).then_inc(l_keep, 1)
                        e.wait_ge(l_keep, n + 1)
                        e.wait_ge(l_sum, n + 2)
                        list_out(n + 1)
                e.wait_ge(m_ytr, n * 4 + 4)
                for j in range(KD):
                    e.wait_ge(m_dn, n * 8 + (j + 1))
                    e.tensor_scalar(yT[:, j, :], bank[2 + j % 2][:, 0:CAP], be[:, 16 + j:17 + j], None, ALU.add)\
                        .then_inc(m_y, 1)
                    if j == 6:
                        for m in range(3):
                            e.wait_ge(g_tr, n * 3 + (m + 4))
                            tokens_out(m)

            with e.Fori(0, NE) as n:
                block_dve(n, n)
            more = e.value_load(it_i[0:1, 1, NI - 1:NI], min_val=0, max_val=NX - 1)
            with e.If(more > 0):
                with e.Fori(NE, more + NE) as n:
                    block_dve(n, e.value_load(it_i[0:1, 0, bass.ds(n, 1)], min_val=0, max_val=NE - 1))


_INS = ["x", "attn_norm_g", "w_in", "ret_norm_g", "sb_q_norm_g", "sb_k_norm_g", "w_out", "ffn_norm_g",
        "w_router", "b_router", "w_gate_up", "b_gate_up", "w_down", "b_down"]


def kernel(**inputs):
    import concourse.bacc as bacc
    from concourse.bass_utils import run_bass_kernel_spmd

    nc = bacc.Bacc("TRN2", target_bir_lowering=False, num_devices=1)
    arrays = {f"in_{name}": np.ascontiguousarray(inputs[name]) for name in _INS}
    arrays["in_consts"], arrays["in_rope"] = constants()
    args = [nc.dram_tensor(n, a.shape, mybir.dt.from_np(a.dtype), kind="ExternalInput").ap() for n, a in arrays.items()]
    args.append(nc.dram_tensor("out_x", (1, S, D), F32, kind="ExternalOutput").ap())
    layer(nc, *args)
    r = run_bass_kernel_spmd(nc, [arrays], core_ids=[0])
    return r.results[0]["out_x"]
```
